# Optimizing a Trainium2 kernel written in Bass

```python
import jax, jax.numpy as jnp
from jax import lax
import numpy as np

D_MODEL = 1024
BATCH = 1
SEQ = 1024
DEPTH = 1
DEC_BATCH = 8
DEC_SEQ = 1
PAST_LEN = 2048
PAGE_SIZE = 128

H_A = 4
HD_A = 64
G_B = 4
CHUNK_B = 128
W_B = 256
H_C = 4
HD_C = 64
DILATED_PAIRS = ((128, 1), (512, 4), (2048, 16))
WINDOW_C = 2048
N_BUCKETS = 32
MAX_DIST = 2048
POOL_WINDOWS = (2, 4, 8, 16)
G_D = 4
C_D = 64
POOL_BUF = 15
N_BRANCH = 4
MIX_W = 256
Q_BLOCK = 128
D_IN = 3 * H_A * HD_A + H_A + 2 * W_B + 3 * H_C * HD_C + G_D * C_D
N_EXPERTS = 16
N_GROUPS = 4
TOP_K = 2
D_EXPERT = 256
ALPHA = (2 * DEPTH) ** 0.25
BETA = (8 * DEPTH) ** -0.25
LN_EPS = 1e-5
NEG_INF = -1e30

kernel_name = 'hybrid_fox_gmlp_dilated_pool_moe_step'

def _in_splits():
    sizes = [H_A * HD_A] * 3 + [H_A] + [W_B] * 2 + [H_C * HD_C] * 3 + [G_D * C_D]
    return [int(s) for s in np.cumsum(sizes)[:-1]]

def _dilation_offsets():
    return np.array([[m * d for m in range(w // d + 1)] for (w, d) in DILATED_PAIRS], dtype=np.int32)

def _t5_buckets(dist):
    exact = N_BUCKETS // 2
    d = np.maximum(dist, 1).astype(np.float32)
    large = exact + (np.log(d / exact) / np.log(MAX_DIST / exact) * (N_BUCKETS - exact)).astype(np.int32)
    large = np.minimum(large, N_BUCKETS - 1)
    return np.where(dist < exact, dist, large).astype(np.int32)

def layer_norm(x, g, b):
    xf = x.astype(jnp.float32)
    mu = xf.mean(-1, keepdims=True)
    var = jnp.square(xf - mu).mean(-1, keepdims=True)
    return ((xf - mu) * lax.rsqrt(var + LN_EPS) * g + b).astype(x.dtype)

def _unblock(o):
    nb, b, qb, h, d = o.shape
    return o.transpose(1, 0, 2, 3, 4).reshape(b, nb * qb, h, d)

def project_in(x, w_in_l, b_forget_l):
    h = x @ w_in_l
    qa, ka, va, fa, ub, vb, qc, kc, vc, pd = jnp.split(h, _in_splits(), axis=-1)
    lead = x.shape[:-1]
    heads = lambda t, n, d: t.reshape(*lead, n, d)
    logf = jax.nn.log_sigmoid(fa.astype(jnp.float32) + b_forget_l.astype(jnp.float32))
    return (heads(qa, H_A, HD_A), heads(ka, H_A, HD_A), heads(va, H_A, HD_A), logf, ub, vb,
            heads(qc, H_C, HD_C), heads(kc, H_C, HD_C), heads(vc, H_C, HD_C), pd)

def fox_attend(q, k, v, fq, fk, qpos):
    logits = jnp.einsum('bqhd,bkhd->bhqk', q, k).astype(jnp.float32) * HD_A ** -0.5
    logits = logits + fq.transpose(0, 2, 1)[..., None] - fk.transpose(0, 2, 1)[:, :, None, :]
    causal = jnp.arange(k.shape[1])[None, :] <= qpos[:, None]
    logits = jnp.where(causal, logits, NEG_INF)
    p = jax.nn.softmax(logits, axis=-1).astype(v.dtype)
    return jnp.einsum('bhqk,bkhd->bqhd', p, v)

def fox_prompt(q, k, v, logf):
    t = q.shape[1]
    f = jnp.cumsum(logf, axis=1)

    def block(s):
        qb = lax.dynamic_slice_in_dim(q, s, Q_BLOCK, 1)
        fq = lax.dynamic_slice_in_dim(f, s, Q_BLOCK, 1)
        return fox_attend(qb, k, v, fq, f, s + jnp.arange(Q_BLOCK))

    return _unblock(lax.map(block, jnp.arange(0, t, Q_BLOCK)))

def dilated_attn(q, k, v, q_rows, bias):
    offs = jnp.asarray(_dilation_offsets())
    n_p, n_m = offs.shape
    b, nq = q.shape[:2]
    rows = q_rows[:, None, None] - offs[None]
    valid = rows >= 0
    rows_c = jnp.maximum(rows, 0).reshape(-1)
    kg = jnp.take(k, rows_c, axis=1).reshape(b, nq, n_p, n_m, H_C, HD_C)
    vg = jnp.take(v, rows_c, axis=1).reshape(b, nq, n_p, n_m, H_C, HD_C)
    logits = jnp.einsum('bqhd,bqpmhd->bqhpm', q, kg).astype(jnp.float32) * HD_C ** -0.5
    logits = logits + bias.transpose(2, 0, 1).astype(jnp.float32)
    logits = jnp.where(valid[None, :, None], logits, NEG_INF)
    lmax = logits.max(-1, keepdims=True)
    e = jnp.exp(logits - lmax)
    s = e.sum(-1, keepdims=True)
    o_p = jnp.einsum('bqhpm,bqpmhd->bqhpd', (e / s).astype(v.dtype), vg)
    lse = (lmax + jnp.log(s))[..., 0]
    w = jax.nn.softmax(lse, axis=-1)
    return jnp.einsum('bqhp,bqhpd->bqhd', w.astype(o_p.dtype), o_p)

def dilated_prompt(q, k, v, bias):
    t = q.shape[1]

    def block(s):
        qb = lax.dynamic_slice_in_dim(q, s, Q_BLOCK, 1)
        return dilated_attn(qb, k, v, s + jnp.arange(Q_BLOCK), bias)

    return _unblock(lax.map(block, jnp.arange(0, t, Q_BLOCK)))

def sgu_inputs(ub, vb, g, b):
    return jax.nn.gelu(ub), layer_norm(jax.nn.gelu(vb), g, b)

def spatial_prompt(v, w_sp, b_sp):
    b, t = v.shape[:2]
    v5 = v.reshape(b, t // CHUNK_B, CHUNK_B, G_B, W_B // G_B)
    m = jnp.einsum('gij,bcjgd->bcigd', jnp.tril(w_sp), v5) + b_sp.T[:, :, None]
    return m.reshape(b, t, W_B)

def spatial_sample(v, w_sp, b_sp):
    b, s = v.shape[:2]
    v4 = v.reshape(b, s, G_B, W_B // G_B)
    m = jnp.einsum('gij,bjgd->bigd', jnp.tril(w_sp)[:, :s, :s], v4) + b_sp[:, :s].T[:, :, None]
    return m.reshape(b, s, W_B)

def pool_mix(p_ext, n_prev, pos0):
    length = p_ext.shape[1]
    cs = jnp.cumsum(p_ext.astype(jnp.float32), axis=1)
    cs = jnp.concatenate([jnp.zeros_like(cs[:, :1]), cs], axis=1)
    j = jnp.arange(n_prev, length)
    pos = pos0 + (j - n_prev)
    means = []
    for g, w in enumerate(POOL_WINDOWS):
        cnt = jnp.minimum(w, pos + 1)
        tot = cs[:, j + 1, g] - cs[:, j + 1 - cnt, g]
        means.append(tot / cnt[None, :, None].astype(jnp.float32))
    mean = jnp.stack(means, axis=2)
    return (mean - p_ext[:, n_prev:].astype(jnp.float32)).astype(p_ext.dtype)

def pool_out(diff, w_pool_l, pool_scale_l):
    lead = diff.shape[:2]
    return jnp.einsum('btgc,gce->btge', diff, w_pool_l).reshape(*lead, G_D * C_D) * pool_scale_l

def merge(x, branches, w_gate_l, b_gate_l, w_branch_l, w_out_l):
    lead = x.shape[:-1]
    gates = jax.nn.sigmoid((x @ w_gate_l).reshape(*lead, N_BRANCH, D_MODEL) + b_gate_l)
    o = jnp.stack(branches, axis=-2)
    br = jnp.einsum('...nw,nwd->...nd', o, w_branch_l)
    return (gates * br).sum(-2) @ w_out_l

def moe(x, w_router, b_router, w1_l, w3_l, w2_l):
    shp = x.shape
    xt = x.reshape(-1, D_MODEL)
    scores = jax.nn.sigmoid((xt @ w_router).astype(jnp.float32))
    sel = scores + b_router.astype(jnp.float32)
    per_g = N_EXPERTS // N_GROUPS
    gscore = lax.top_k(sel.reshape(-1, N_GROUPS, per_g), TOP_K)[0].sum(-1)
    gidx = jnp.argmax(gscore, axis=-1)
    in_grp = (jnp.arange(N_EXPERTS) // per_g)[None, :] == gidx[:, None]
    _, eidx = lax.top_k(jnp.where(in_grp, sel, NEG_INF), TOP_K)
    gw = jnp.take_along_axis(scores, eidx, axis=-1)
    gw = gw / gw.sum(-1, keepdims=True)
    gate = (jax.nn.one_hot(eidx, N_EXPERTS, dtype=jnp.float32) * gw[..., None]).sum(1)
    out = jnp.zeros(xt.shape, jnp.float32)
    for e in range(N_EXPERTS):
        h = jax.nn.silu(xt @ w1_l[e]) * (xt @ w3_l[e])
        out = out + gate[:, e:e + 1] * (h @ w2_l[e])
    return out.astype(x.dtype).reshape(shp)

def mixer_prompt(x, c_bias, mw):
    (w_in_l, b_forget_l, sgu_g_l, sgu_b_l, w_sp_l, b_sp_l, w_pool_l, pool_scale_l,
     w_gate_l, b_gate_l, w_branch_l, w_out_l) = mw
    b, t = x.shape[:2]
    qa, ka, va, logf, ub, vb, qc, kc, vc, pd = project_in(x, w_in_l, b_forget_l)
    o_a = fox_prompt(qa, ka, va, logf).reshape(b, t, H_A * HD_A)
    u, v = sgu_inputs(ub, vb, sgu_g_l, sgu_b_l)
    o_b = u * spatial_prompt(v, w_sp_l, b_sp_l)
    o_c = dilated_prompt(qc, kc, vc, c_bias).reshape(b, t, H_C * HD_C)
    o_d = pool_out(pool_mix(pd.reshape(b, t, G_D, C_D), 0, 0), w_pool_l, pool_scale_l)
    y = merge(x, [o_a, o_b, o_c, o_d], w_gate_l, b_gate_l, w_branch_l, w_out_l)
    wb = min(WINDOW_C, t)
    n_pg = t // PAGE_SIZE
    state = (ka.reshape(b, n_pg, PAGE_SIZE, H_A, HD_A), va.reshape(b, n_pg, PAGE_SIZE, H_A, HD_A),
             logf.reshape(b, n_pg, PAGE_SIZE, H_A), kc[:, t - wb:], vc[:, t - wb:], pd[:, t - POOL_BUF:])
    return y, state

def mixer_sample(x, cache_k_l, cache_v_l, cache_logf_l, state_k_l, state_v_l, state_pool_l, page_table, c_bias, mw):
    (w_in_l, b_forget_l, sgu_g_l, sgu_b_l, w_sp_l, b_sp_l, w_pool_l, pool_scale_l,
     w_gate_l, b_gate_l, w_branch_l, w_out_l) = mw
    db, s = x.shape[:2]
    n_past = page_table.shape[1] * PAGE_SIZE
    qa, ka, va, logf, ub, vb, qc, kc, vc, pd = project_in(x, w_in_l, b_forget_l)
    k_past = cache_k_l[page_table].reshape(db, n_past, H_A, HD_A)
    v_past = cache_v_l[page_table].reshape(db, n_past, H_A, HD_A)
    lf_past = cache_logf_l[page_table].reshape(db, n_past, H_A).astype(jnp.float32)
    k_all = jnp.concatenate([k_past, ka.astype(k_past.dtype)], axis=1)
    v_all = jnp.concatenate([v_past, va.astype(v_past.dtype)], axis=1)
    f = jnp.cumsum(jnp.concatenate([lf_past, logf], axis=1), axis=1)
    o_a = fox_attend(qa, k_all, v_all, f[:, n_past:], f, n_past + jnp.arange(s)).reshape(db, s, H_A * HD_A)
    u, v = sgu_inputs(ub, vb, sgu_g_l, sgu_b_l)
    o_b = u * spatial_sample(v, w_sp_l, b_sp_l)
    wb = state_k_l.shape[1]
    k_ext = jnp.concatenate([state_k_l, kc.astype(state_k_l.dtype)], axis=1)
    v_ext = jnp.concatenate([state_v_l, vc.astype(state_v_l.dtype)], axis=1)
    o_c = dilated_attn(qc, k_ext, v_ext, wb + jnp.arange(s), c_bias).reshape(db, s, H_C * HD_C)
    n_prev = state_pool_l.shape[1]
    p_ext = jnp.concatenate([state_pool_l.astype(pd.dtype), pd], axis=1).reshape(db, n_prev + s, G_D, C_D)
    o_d = pool_out(pool_mix(p_ext, n_prev, n_past), w_pool_l, pool_scale_l)
    y = merge(x, [o_a, o_b, o_c, o_d], w_gate_l, b_gate_l, w_branch_l, w_out_l)
    state = (ka, va, logf, kc, vc, pd, v)
    return y, state

def setup_inputs(seed: int = 0) -> dict:
    key = jax.random.key(seed)
    k = jax.random.split(key, 32)
    nrm = lambda i, shape, scale=1.0: jax.random.normal(k[i], shape, jnp.float32) * scale
    n_pages = PAST_LEN // PAGE_SIZE
    n_used = DEC_BATCH * n_pages
    n_pool = n_used + max(1, n_used // 4)
    wb = min(WINDOW_C, PAST_LEN)
    page_table = jax.random.permutation(k[8], n_pool)[:n_used].reshape(DEC_BATCH, n_pages).astype(jnp.int32)
    return {
        'x_prompt': nrm(0, (BATCH, SEQ, D_MODEL)),
        'x_sample': nrm(1, (DEC_BATCH, DEC_SEQ, D_MODEL)),
        'cache_k_a': nrm(2, (DEPTH, n_pool, PAGE_SIZE, H_A, HD_A)),
        'cache_v_a': nrm(3, (DEPTH, n_pool, PAGE_SIZE, H_A, HD_A)),
        'cache_logf_a': jax.nn.log_sigmoid(2.5 + nrm(4, (DEPTH, n_pool, PAGE_SIZE, H_A))),
        'state_k_c': nrm(5, (DEPTH, DEC_BATCH, wb, H_C, HD_C)),
        'state_v_c': nrm(6, (DEPTH, DEC_BATCH, wb, H_C, HD_C)),
        'state_pool_d': nrm(7, (DEPTH, DEC_BATCH, POOL_BUF, G_D * C_D)),
        'page_table': page_table,
        'w_in': nrm(9, (DEPTH, D_MODEL, D_IN), D_MODEL ** -0.5),
        'b_forget': jax.random.uniform(k[10], (DEPTH, H_A), jnp.float32, 1.0, 4.0),
        'sgu_ln_g': 1.0 + nrm(11, (DEPTH, W_B), 0.1),
        'sgu_ln_b': nrm(12, (DEPTH, W_B), 0.1),
        'w_spatial': nrm(13, (DEPTH, G_B, CHUNK_B, CHUNK_B), CHUNK_B ** -0.5),
        'b_spatial': 1.0 + nrm(14, (DEPTH, G_B, CHUNK_B), 0.1),
        't5_table': nrm(15, (N_BUCKETS, H_C), 0.5),
        'w_pool': nrm(16, (DEPTH, G_D, C_D, C_D), C_D ** -0.5),
        'pool_scale': 1.0 + nrm(17, (DEPTH, G_D * C_D), 0.1),
        'w_gate': nrm(18, (DEPTH, D_MODEL, N_BRANCH * D_MODEL), D_MODEL ** -0.5),
        'b_gate': nrm(19, (DEPTH, N_BRANCH, D_MODEL), 0.1),
        'w_branch': nrm(20, (DEPTH, N_BRANCH, MIX_W, D_MODEL), MIX_W ** -0.5 * BETA),
        'w_out': nrm(21, (DEPTH, D_MODEL, D_MODEL), D_MODEL ** -0.5 * BETA),
        'ln1_g': 1.0 + nrm(22, (DEPTH, D_MODEL), 0.1),
        'ln1_b': nrm(23, (DEPTH, D_MODEL), 0.1),
        'w_router': nrm(24, (D_MODEL, N_EXPERTS), D_MODEL ** -0.5),
        'b_router': nrm(25, (N_EXPERTS,), 0.01),
        'w1': nrm(26, (DEPTH, N_EXPERTS, D_MODEL, D_EXPERT), D_MODEL ** -0.5),
        'w3': nrm(27, (DEPTH, N_EXPERTS, D_MODEL, D_EXPERT), D_MODEL ** -0.5),
        'w2': nrm(28, (DEPTH, N_EXPERTS, D_EXPERT, D_MODEL), D_EXPERT ** -0.5 * BETA),
        'ln2_g': 1.0 + nrm(29, (DEPTH, D_MODEL), 0.1),
        'ln2_b': nrm(30, (DEPTH, D_MODEL), 0.1),
    }

def reference(x_prompt, x_sample, cache_k_a, cache_v_a, cache_logf_a, state_k_c, state_v_c, state_pool_d,
              page_table, w_in, b_forget, sgu_ln_g, sgu_ln_b, w_spatial, b_spatial, t5_table, w_pool,
              pool_scale, w_gate, b_gate, w_branch, w_out, ln1_g, ln1_b, w_router, b_router, w1, w3, w2,
              ln2_g, ln2_b):
    c_bias = t5_table[jnp.asarray(_t5_buckets(_dilation_offsets()))]
    yp, ys = x_prompt, x_sample
    sp, ss = [], []
    for l in range(DEPTH):
        mw = (w_in[l], b_forget[l], sgu_ln_g[l], sgu_ln_b[l], w_spatial[l], b_spatial[l], w_pool[l],
              pool_scale[l], w_gate[l], b_gate[l], w_branch[l], w_out[l])
        mp, st_p = mixer_prompt(yp, c_bias, mw)
        yp = layer_norm(ALPHA * yp + mp, ln1_g[l], ln1_b[l])
        yp = layer_norm(ALPHA * yp + moe(yp, w_router, b_router, w1[l], w3[l], w2[l]), ln2_g[l], ln2_b[l])
        ms, st_s = mixer_sample(ys, cache_k_a[l], cache_v_a[l], cache_logf_a[l], state_k_c[l], state_v_c[l],
                                state_pool_d[l], page_table, c_bias, mw)
        ys = layer_norm(ALPHA * ys + ms, ln1_g[l], ln1_b[l])
        ys = layer_norm(ALPHA * ys + moe(ys, w_router, b_router, w1[l], w3[l], w2[l]), ln2_g[l], ln2_b[l])
        sp.append(st_p)
        ss.append(st_s)
    stk = lambda sts, i: jnp.stack([st[i] for st in sts])
    return (yp, ys, stk(sp, 0), stk(sp, 1), stk(sp, 2), stk(ss, 0), stk(ss, 1), stk(ss, 2),
            stk(sp, 3), stk(sp, 4), stk(ss, 3), stk(ss, 4), stk(sp, 5), stk(ss, 5), stk(ss, 6))


_drawn_inputs = setup_inputs


def setup_inputs(seed=0):
    import zlib

    import numpy as np

    out = dict(_drawn_inputs(seed))
    spreads = {}
    factors = {'cache_logf_a': 62.387,
     'state_k_c': 3.855,
     'state_v_c': 3.183,
     'b_spatial': 3.109,
     'b_gate': 2.849}
    for name, (base, spread) in spreads.items():
        noise = np.random.default_rng([zlib.crc32(name.encode()), seed]).standard_normal(out[name].shape)
        drawn = base * np.exp(spread * noise) if base else spread * noise
        out[name] = __import__('jax').numpy.asarray(drawn.astype(out[name].dtype))
    for name, factor in factors.items():
        out[name] = (out[name] * factor).astype(out[name].dtype)
    return out
```

```python
import math
from contextlib import ExitStack

import numpy as np
import concourse.bass as bass
from concourse import mybir

F32 = mybir.dt.float32
F32R = mybir.dt.float32r
I32 = mybir.dt.int32
U32 = mybir.dt.uint32
ALU = mybir.AluOpType
ACT = mybir.ActivationFunctionType
AX = mybir.AxisListType

P = 128
D = 1024
KD = D // P
SEQ = 1024
NT = SEQ // P
NB = 8
TOK = SEQ + NB
CH = TOK // 3
PAST = 2048
PAGES = PAST // P
H = 4
HD = 64
W = 256
NE = 16
NG = 4
FE = 256
ALPHA = 2.0 ** 0.25
EPS = 1e-5
NEG = -1e30
SCALE = HD ** -0.5
WINDOWS = (2, 4, 8, 16)
DILATED = ((128, 1), (512, 4), (2048, 16))
NBUCK = 32
MOE_TILES = (2 * TOK - NE) // P + NE
SLOTS = MOE_TILES * P
TBW = SEQ + P
WM = D + W
CHUNKS = {"uv": (772, 512), "qka": (0, 512), "vfa": (512, 260), "qkc": (1284, 512), "vpd": (1796, 512)}
ORDER = ("uv", "qka", "vfa", "qkc", "vpd")
TILE_ORDER = (8, 0, 1, 2, 3, 4, 5, 6, 7)
SC = {"qka": 0, "vfa": 512, "qkc": 772, "vpd": 1284}
SW = 1796


def rows(t):
    return P if t < NT else NB


def build(nc, a):
    ctx = ExitStack()
    with ctx:
        names = [0]
        BASE = 16512

        def at(off, shape, dt=F32):
            names[0] += 1
            return ctx.enter_context(placed(nc, f"b{names[0]}_{off}", shape, dt, BASE + off))

        sems = {}

        def S(name):
            if name not in sems:
                sems[name] = ctx.enter_context(nc.semaphore(name))
            return sems[name]

        TOKB = KD * TOK * 4
        XT, OT, MT, RING = 0, TOKB, 2 * TOKB, 3 * TOKB
        RINGB = TOKB + 8192
        QK = RING + RINGB
        VR = QK + 16384
        PD = VR + 8192
        BI = PD + 8192
        TMP = BI + 16384
        xT = at(XT, [P, KD, TOK])
        oT = at(OT, [P, 4, 2, TOK])
        mT = at(MT, [P, KD, TOK])
        w_ring = at(RING, [P, 2, KD, 512])
        p_T = at(RING + TOKB, [P, 2, SEQ])
        uv = at(QK, [P, NT + 1, 512])
        qT = at(QK, [P, 2, SEQ])
        kT = at(QK + 8192, [P, 2, SEQ])
        va = at(VR, [P, NT, W])
        vp = at(VR, [P, NT, 512])
        fb = at(BI, [P, H, SEQ])
        tb = at(BI, [P, H, SEQ])
        gbB = at(BI, [P, 2, W])
        st_s = at(BI + 5120, [P, W])
        wsp = at(BI + 2048, [P, 4, P])
        trilB = at(BI + 4096, [P, P])
        s_nat = at(TMP, [P, SW])
        o = TMP + SW * 4
        ident = at(o, [P, P]); o += 512
        nat = at(o, [P, 2, 512]); NAT = o; o += 4096
        o_nat = nat
        p_sb = at(o, [P, 2, SEQ]); PSB = o; o += 8192
        causal = at(o, [P, P]); o += 512
        bsp = at(o, [P, 4]); o += 16
        bfb = at(o, [P, H]); o += 16
        fa = at(o, [P, NT + 1, H]); o += 144
        faz = at(o, [P, NT + 1, H]); o += 144
        fae = at(o, [P, NT + 1, H]); o += 144
        fal = at(o, [P, NT + 1, H]); o += 144
        lf = at(o, [P, NT + 1, H]); o += 144
        lpre = at(o, [P, NT, H]); o += 128
        st6 = at(o, [P, 2, 6]); o += 48
        mv = at(o, [P, NT + 1, 2]); o += 80
        rs = at(o, [P, NT + 1]); o += 48
        rs2 = at(o, [P, NT + 1]); o += 48
        swb = at(o, [P, 2, 4]); o += 32
        am = at(o, [P, 4]); o += 16
        asum = at(o, [P, 4]); o += 16
        arec = at(o, [P, 4]); o += 16
        lgb = at(o, [P, 32]); o += 128
        psc = at(o, [P, 2]); o += 16
        assert BASE + o <= 229368, BASE + o
        o = MT
        kv = at(o, [P, 2, 9, W]); o += 18432
        qb = at(o, [P, 2, W]); o += 2048
        sA = at(o, [P, NB, 17, H]); o += 2176
        sC = at(o, [P, NB, 4, H]); o += 512
        lfg = at(o, [P, NB, 16, H]); o += 2048
        lfs = at(o, [P, 2, NB, 16, H]); o += 4096
        idx = at(o, [P, NB, 4], U32); o += 128
        ptb = at(o, [P, NB], I32); o += 32
        ptk = at(o, [P, 4]); o += 16
        bC = at(o, [P, 4, H]); o += 64
        bNew = at(o, [P, 1]); o += 32
        mx = at(o, [P, P]); o += 512
        mcol = at(o, [P, 1]); o += 32
        mrow = at(o, [P, 32]); o += 128
        dsum = at(o, [P, 32]); o += 128
        drec = at(o, [P, 32]); o += 128
        ltot = at(o, [P, 32]); o += 128
        trisA = at(o, [P, P]); o += 512
        ones = at(o, [P, P]); o += 512
        assert o <= RING, (o, RING)
        oh_rev = at(OT, [NBUCK + 1, TBW])
        tb_src = at(OT + 4608, [P, 4, TBW])
        oh_dec = at(OT + 23040, [NBUCK + 1, 4, P])
        t5 = at(OT + 25088, [NBUCK + 1, H])
        tri_neg = at(OT + 25600, [P, P])
        ones_neg = at(OT + 26112, [P, P])
        bands = at(PSB, [P, 4, 3, P])
        wpb = at(PSB + 6144, [P, 2, P])
        dT = at(BI, [P, 2, TOK])
        sd = at(PSB + 7168, [P, W])
        spool = at(RING + 16384, [P, 16, W])

        ps = ctx.enter_context(nc.psum_tensor("ps", [P, 8, 512], F32))


        def pj_index(chunk, t):
            return ORDER.index(chunk) * 9 + TILE_ORDER.index(t)

        items = [(qb_, h) for qb_ in range(NT) for h in range(H)]

        PT_USES = [[], []]
        OUT_DONE = []
        used = [0, 0]
        for br in range(2):
            for qt, _h in items:
                PT_USES[br].append(tuple(used))
                used[0] += 1
                used[1] += qt >= 4
                used[0] += _h == 1 and qt > 0
            used[0] += 1
            OUT_DONE.append(used[0])
        OUT_USES = [[PT_USES[br][4 * (qt + 1) + 1][0] + 1 for qt in range(NT - 1)] + [OUT_DONE[br] - 1] for br in range(2)]
        PTC = (OUT_DONE[0], len(items) // 2)
        VD_A = [16 * (b + 1) * (1 + half) for b in range(NB) for half in range(2)]
        VD_C = [16 * NB * (1 + b % 2) + 64 * (b // 2 + 1) for b in range(NB)]

        xH, xL = at(RING, [P, KD, TOK], F32R), at(XT, [P, KD, TOK], F32R)
        oH, oL = at(QK, [P, 4, 2, TOK], F32R), at(OT, [P, 4, 2, TOK], F32R)
        wg, wL = at(BI + 4608, [P, 2, WM + 1]), at(BI + 4608, [P, 2, WM + 1], F32R)
        wH = [at(RING + TOKB, [P, WM], F32R), at(PSB, [P, WM], F32R)]
        assert BI + 4608 + 8 * (WM + 1) <= TMP and 8 * WM // 2 + 512 <= 8192
        sg = at(BI + 256, [P, 2, CH])
        prod = at(BI + 256 + 8 * CH, [P, CH])
        wo = [at(QK, [P, KD, 512]), at(OT, [P, KD, 512])]
        ln1 = [at(TMP, [P, D]), at(NAT, [P, D])]
        wr = at(PSB + 4 * WM, [P, KD, NE])
        acc = at(RING, [P, NT + 1, D])
        xin = at(OT + 16384, [P, 2, D])
        xg = at(OT + 8192, [P, 2, D])
        xgT = at(OT + 16384, [P, 2, KD, P])
        x1T = at(OT + 24576, [P, KD, P])
        w13 = at(QK, [P, 2, KD, 512])
        w2 = at(BI, [P, 2, 2, D])
        yo = at(XT, [P, 2, D])
        hs = at(XT + 8192, [P, 2, FE])
        hn = at(XT + 10240, [P, 2, FE])
        hT = at(XT + 12288, [P, 2, 2, P])
        ln2 = at(XT + 14336, [P, 2, D])
        yg = at(MT, [P, 4, 2, D])
        o = XT + 22528
        rt = {}
        for nm, shape, dt in (("s", [P, 9, 16], F32), ("sel", [P, 9, 16], F32), ("chosen", [P, 9, 16], F32),
                              ("gsc", [P, 9, 4], F32), ("gin", [P, 9, 4], F32),
                              ("gate", [P, 9, 16], F32), ("gsum", [P, 9], F32),
                              ("pos", [P, 9, 16], F32), ("pre", [P, 9, 16], F32), ("ne", [P, 16], F32),
                              ("nt", [P, 16], F32), ("inc", [P, 2, 16], F32), ("tmp", [P, 9, 16], F32),
                              ("slotf", [P, 2, 9], F32), ("slot", [P, 9, 2], U32), ("gw", [P, 9, 2], F32),
                              ("te", [P, 32], F32), ("tei", [P, 32], I32), ("brow", [P, 16], F32)):
            rt[nm] = at(o, shape, dt)
            o += 4 * int(np.prod(shape[1:]))
            o += -o % 32
        assert o <= OT, (o, OT)
        cmp = at(MT + 16384, [P, 36, 4, 4])
        o = OT + 28672
        cmp32 = at(MT + 16384, [P, 32, 16])
        before = at(o, [P, P]); o += 512
        ones2 = at(o, [P, P]); o += 512
        valid = at(o, [P, NT + 1]); o += 64
        tok = at(o, [P, NT + 1], I32); o += 64
        tileno = at(o, [P, 32]); o += 128
        zid = at(o, [P, 32], I32); o += 128
        idall = at(o, [P, 32], I32); o += 128
        idt = at(o, [P, 2], I32); o += 32
        st12 = at(o, [P, 2, 6]); o += 64
        mv2 = at(o, [P, 2]); o += 32
        rv = at(o, [P, 2]); o += 32
        fs = at(o, [P, 4, 8]); o += 128
        assert o <= MT

        def emit_sp2(sp):
            with sp.Fori(0, 2 * KD) as i:
                for u in range(2):
                    w0 = sp.snap(i * 2 + (1 + u), min_val=1, max_val=4 * KD)
                    src = a["w_merge"][bass.ds(i * 2 + u, 1)].rearrange("a p n -> (a p) n")
                    sp.wait_ge(S("merge_free"), w0)
                    sp.dma_start(wg[:, u, :], src).then_inc(S(f"wg{u}"), 16)
            sp.dma_start(ln1[0][:], a["ln1_g"].to_broadcast([P, D])).then_inc(S("wo"), 16)
            sp.dma_start(ln1[1][:], a["ln1_b"].to_broadcast([P, D])).then_inc(S("wo"), 16)
            sp.dma_start(wr[:], a["w_router"]).then_inc(S("wo"), 16)
            sp.wait_ge(S("mb"), 12 * (KD - 1) + 6)
            for n in range(2):
                sp.dma_start(wo[n][:], a["w_out"][:, :, n * 512:n * 512 + 512]).then_inc(S("wo"), 16)
            sp.wait_ge(S("merged"), 1)
            for t in range(NT + 1):
                r = rows(t)
                if t >= 2:
                    sp.wait_ge(S("z"), t - 1)
                sp.dma_start(xin[0:r, t % 2, :], a["x"][t * P:t * P + r, :]).then_inc(S(f"xin{t % 2}"), 16)
                if t == 1:
                    for nm, dst in (("before", before), ("valid", valid), ("token", tok), ("tileno", tileno)):
                        sp.dma_start(dst[:], a[nm]).then_inc(S("rc"), 16)
                    sp.dma_start(rt["brow"][:], a["b_router"].to_broadcast([P, NE])).then_inc(S("rc"), 16)
                    sp.dma_start(ln2[:, 0, :], a["ln2_g"].to_broadcast([P, D])).then_inc(S("rc"), 16)
                    sp.dma_start(ln2[:, 1, :], a["ln2_b"].to_broadcast([P, D])).then_inc(S("rc"), 16)
                    sp.wait_ge(S("zeroed"), 1)
                    sp.dma_start(a["ids"].rearrange("(p n) o -> p (n o)", p=P), zid[:]).then_inc(S("ids0"), 16)
            for t in range(NT + 1):
                r = rows(t)
                sp.wait_ge(S("x1"), t + 1)
                sp.dma_start(a["x1"][t * P:t * P + r, :], acc[0:r, t, :]).then_inc(S("x1d"), 16)
            sp.wait_ge(S("routed"), 1)
            with sp.Fori(0, MOE_TILES // 2) as i:
                for u in range(2):
                    e = sp.value_load(rt["tei"][0:1, bass.ds(i * 2 + u, 1)], min_val=0, max_val=NE - 1)
                    n = sp.snap(i * 2 + (u + 1), min_val=1, max_val=MOE_TILES)
                    src = a["w13"][bass.ds(e, 1)].rearrange("a p n -> (a p) n")
                    src2 = a["w2"][bass.ds(e, 1)].rearrange("a p n -> (a p) n")
                    sp.wait_ge(S("w13_free"), n)
                    sp.dma_start(w13[:, u].rearrange("p k n -> p (k n)"), src).then_inc(S(f"w13_{u}"), 16)
                    sp.wait_ge(S("w2_free"), n)
                    sp.dma_start(w2[:, u].rearrange("p k n -> p (k n)"), src2).then_inc(S(f"w2_{u}"), 16)
            for t in range(NT + 1):
                r = rows(t)
                sp.wait_ge(S("y_ready"), t + 1)
                dst = a["y_p"][t * P:(t + 1) * P, :] if t < NT else a["y_s"]
                sp.dma_start(dst, acc[0:r, t, :]).then_inc(S("out"), 16)
            sp.wait_ge(S("out"), 16 * (5 + NT + 1))
            for nm in ("st0", "st1"):
                sp.wait_ge(S(nm), 16 * NT)
            for nm in ("out_pool", "out_vc", "out_va", "out_vb"):
                sp.wait_ge(S(nm), 16)
            sp.wait_ge(S("out_lf"), 32)

        def emit_pe2(pe, mm, tr):
            pe.wait_ge(S("so"), 3)
            def merge_chunk(i):
                for n in range(4):
                    pe.wait_ge(S("wsplit"), i * 8 + (2 * n + 2))
                    for c in range(3):
                        j = 3 * n + c
                        s = (j % 2) * 2
                        tk = slice(c * CH, (c + 1) * CH)
                        pe.wait_ge(S("mp"), i * 12 + (j + 1))
                        hi, lo = wH[n % 2], wL[:, n % 2, :]
                        for k in range(KD):
                            w = slice(k * P, (k + 1) * P)
                            mm(ps[:, s, 0:CH], hi[:, w], xH[:, k, tk], start=(k == 0), stop=False)
                            mm(ps[:, s, 0:CH], hi[:, w], xL[:, k, tk], start=False, stop=False)
                            m = mm(ps[:, s, 0:CH], lo[:, w], xH[:, k, tk], start=False, stop=(k == KD - 1))
                        m.then_inc(S("mg"), 1)
                        for f in range(2):
                            w = slice(D + f * P, D + (f + 1) * P)
                            mm(ps[:, s + 1, 0:CH], hi[:, w], oH[:, n, f, tk], start=(f == 0), stop=False)
                            mm(ps[:, s + 1, 0:CH], hi[:, w], oL[:, n, f, tk], start=False, stop=False)
                            m = mm(ps[:, s + 1, 0:CH], lo[:, w], oH[:, n, f, tk], start=False, stop=(f == 1))
                        m.then_inc(S("mb"), 1)

            with pe.Fori(0, KD) as i:
                merge_chunk(i)
            pe.wait_ge(S("wo"), 80)
            pe.wait_ge(S("macc"), 72)

            def y_tile(t):
                r = rows(t)
                if t >= 2:
                    pe.wait_ge(S("z"), t - 1)
                for n in range(2):
                    for k in range(KD):
                        m = mm(ps[0:r, (t % 2) * 2 + n, :], mT[:, k, t * P:t * P + r], wo[n][:, k, :],
                               start=(k == 0), stop=(k == KD - 1))
                m.then_inc(S("y1"), 1)

            def route(t):
                r = rows(t)
                pe.wait_ge(S("x1"), t + 1)
                if t:
                    pe.wait_ge(S("x1T"), t)
                for k in range(KD):
                    m = tr(ps[:, 4 + k // 4, (k % 4) * P:(k % 4) * P + r], acc[0:r, t, k * P:(k + 1) * P], r)
                m.then_inc(S("x1tr"), 1)
                pe.wait_ge(S("x1T"), t + 1)
                for k in range(KD):
                    m = mm(ps[0:r, 6, t * NE:(t + 1) * NE], x1T[:, k, 0:r], wr[:, k, :],
                           start=(k == 0), stop=(k == KD - 1))
                m.then_inc(S("lg"), 1)

            for t in range(NT + 1):
                y_tile(t)
                if t:
                    route(t - 1)
            route(NT)
            pe.wait_ge(S("mask"), 1)
            m_ = rt["chosen"][:].rearrange("p t e -> p (t e)")
            mm(ps[:, 7, 0:144], before[:], m_, start=True, stop=True)
            mm(ps[:, 7, 256:400], ones2[:], m_, start=True, stop=True).then_inc(S("pos"), 1)

            def x_transposes(u, n):
                pe.wait_ge(S(f"xg{u}"), n[1])
                pe.wait_ge(S("xga_free"), n[0])
                for k in range(4):
                    m = tr(ps[:, 4, k * P:(k + 1) * P], xg[:, u, k * P:(k + 1) * P])
                m.then_inc(S("xtra"), 1)
                pe.wait_ge(S("xgb_free"), n[0])
                for k in range(4):
                    m = tr(ps[:, 5, k * P:(k + 1) * P], xg[:, u, (k + 4) * P:(k + 5) * P])
                m.then_inc(S("xtrb"), 1)

            def hidden(u, n):
                pe.wait_ge(S(f"w13_{u}"), n[1])
                pe.wait_ge(S("xga"), n[0])
                pe.wait_ge(S("xgb"), n[0])
                pe.wait_ge(S("h_free"), n[0])
                for k in range(KD):
                    m = mm(ps[:, u, :], xgT[:, u, k, :], w13[:, u, k, :], start=(k == 0), stop=(k == KD - 1))
                m.then_inc(S("hid"), 1)

            def down(u, n, between):
                pe.wait_ge(S("h"), n[0])
                pe.wait_ge(S("hT"), n[2])
                for f in range(2):
                    m = tr(ps[:, 6, f * P:(f + 1) * P], hn[:, u, f * P:(f + 1) * P])
                m.then_inc(S("htr"), 1)
                between()
                pe.wait_ge(S("hT"), n[3])
                pe.wait_ge(S(f"w2_{u}"), n[1])
                for c in range(2):
                    pe.wait_ge(S("ya" if c == 0 else "yb"), n[0])
                    for f in range(2):
                        m = mm(ps[:, 2 + c, :], hT[:, u, f, :], w2[:, u, f, c * 512:(c + 1) * 512],
                               start=(f == 0), stop=(f == 1))
                    m.then_inc(S("dna" if c == 0 else "dnb"), 1)

            def vals(i, k):
                T = i * 2 + k
                return (T + 1, (i + k // 2 + 1) * 16, T + 1, T + 2)

            pe.wait_ge(S("routed"), 1)
            x_transposes(0, vals(0, 0))
            x_transposes(1, vals(0, 1))
            hidden(0, vals(0, 0))
            with pe.Fori(0, MOE_TILES // 2 - 1) as i:
                for u in range(2):
                    hidden(1 - u, vals(i, u + 1))
                    down(u, vals(i, u), lambda: x_transposes(u, vals(i, u + 2)))
            i = MOE_TILES // 2 - 1
            hidden(1, vals(i, 1))
            down(0, vals(i, 0), lambda: None)
            down(1, vals(i, 1), lambda: None)

        def emit_act2(act):
            with act.Fori(0, KD) as i:
                for j in range(12):
                    bias = wg[:, (j // 3) % 2, WM:WM + 1]
                    act.wait_ge(S("mp"), i * 12 + (j + 1))
                    act.wait_ge(S("mg"), i * 12 + (j + 1))
                    act.activation(sg[:, j % 2, :], ps[:, (j % 2) * 2, 0:CH], ACT.Sigmoid, bias=bias
                                   ).then_inc(S("sgd"), 1)
            for t in range(NT + 1):
                act.wait_ge(S("var"), t + 2)
                act.activation(rv[:, 1:2], rv[:, 0:1], ACT.Sqrt).then_inc(S("sd"), 1)
                if t:
                    evict_x1T(act, t - 1)
            evict_x1T(act, NT)
            act.wait_ge(S("lg"), NT + 1)
            act.wait_ge(S("zeroed"), 2)
            act.activation(rt["s"][:, 0:NT, :].rearrange("p t e -> p (t e)"), ps[:, 6, 0:NT * NE], ACT.Sigmoid)
            act.activation(rt["s"][0:NB, NT, :], ps[0:NB, 6, NT * NE:(NT + 1) * NE], ACT.Sigmoid).then_inc(S("score"), 1)

            def rows_T(u, n):
                act.wait_ge(S("xtra"), n[0])
                act.copy(xgT[:, u, 0:4, :].rearrange("p k r -> p (k r)"), ps[:, 4, :]).then_inc(S("xga"), 1)
                act.wait_ge(S("xga"), n[0])
                act.sem_inc(S("xga_free"), 1)

            def silu(u, n):
                act.wait_ge(S("hid"), n[0])
                act.wait_ge(S("h"), n[4])
                act.activation(hs[:, u, :], ps[:, u, 0:FE], ACT.Silu).then_inc(S("hs"), 1)

            def out_a(u, n, T):
                act.wait_ge(S("dna"), n[0])
                act.wait_ge(S(f"ys{u}"), n[5])
                act.copy(yo[:, u, 0:512], ps[:, 2, :]).then_inc(S("ya"), 1)
                dst = a["yd"][bass.ds(T * P, P), :] if not isinstance(T, int) else a["yd"][T * P:(T + 1) * P, :]
                act.wait_ge(S("yb"), n[1])
                act.wait_ge(S("ya"), n[1])
                act.dma_start(dst, yo[:, u, :]).then_inc(S(f"ys{u}"), 16)

            def vals(i, k):
                T = i * 2 + k
                return (T + 1, T + 2, None, None, T, (i + k // 2) * 16 + 16)

            act.wait_ge(S("x1d"), 16 * (NT + 1))
            for t in range(NT + 1):
                act.mul(acc[0:rows(t), t, :], acc[0:rows(t), t, :], ALPHA).then_inc(S("acc_act"), 1)
            act.wait_ge(S("routed"), 1)
            rows_T(0, vals(0, 0))
            rows_T(1, vals(0, 1))
            act.wait_ge(S("hid"), 1)
            act.activation(hs[:, 0, :], ps[:, 0, 0:FE], ACT.Silu).then_inc(S("hs"), 1)
            with act.Fori(0, MOE_TILES // 2 - 1) as i:
                for u in range(2):
                    silu(1 - u, vals(i, u + 1))
                    rows_T(u, vals(i, u + 2))
                    out_a(u, vals(i, u), i * 2 + u)
            i = MOE_TILES // 2 - 1
            silu(1, vals(i, 1))
            out_a(0, vals(i, 0), i * 2)
            out_a(1, vals(i, 1), i * 2 + 1)
            for t in range(NT + 2):
                if t <= NT:
                    r = rows(t)
                    act.wait_ge(S("var"), NT + 1 + t + 2)
                    act.activation(fs[0:r, t % 4, 3:4], fs[0:r, t % 4, 2:3], ACT.Sqrt).then_inc(S("sd"), 1)
                if t:
                    r = rows(t - 1)
                    act.wait_ge(S("fsd"), t)
                    act.activation(acc[0:r, t - 1, :], acc[0:r, t - 1, :], ACT.Identity, scale=fs[0:r, (t - 1) % 4, 4:5],
                                   bias=fs[0:r, (t - 1) % 4, 5:6]).then_inc(S("acc_act"), 1)

        def evict_x1T(eng, t):
            r = rows(t)
            eng.wait_ge(S("x1tr"), t + 1)
            if t:
                eng.wait_ge(S("lg"), t)
            eng.copy(x1T[:, :, 0:r], ps[:, 4:6, :].rearrange("p a b -> p (a b)").rearrange("p (k r) -> p k r", r=P)[:, :, 0:r]
                     ).then_inc(S("x1T"), 1)

        def norm_stats(dve, link, z, r, n):
            for c in range(2):
                m = dve.bn_stats(st12[0:r, c, :], z[:, c * 512:(c + 1) * 512])
            link(m)
            link(dve.bn_aggr(mv2[0:r, :], st12[0:r].rearrange("p c s -> p (c s)")))
            dve.tensor_scalar(rv[0:r, 0:1], mv2[0:r, 1:2], EPS, None, ALU.add).then_inc(S("var"), 1)
            dve.wait_ge(S("sd"), n + 2)
            link(dve.reciprocal(rv[0:r, 0:1], rv[0:r, 1:2]))

        def emit_dve2(dve, link):
            dve.sem_inc(S("mp"), 2)
            def split_weights(g, wait, high_done):
                dve.wait_ge(S(f"wg{g}"), wait)
                dve.tensor_copy(wH[g][:], wg[:, g, 0:WM]).then_inc(S("wsplit"), 1)
                dve.wait_ge(S("wsplit"), high_done)
                dve.tensor_tensor(wL[:, g, 0:WM], wg[:, g, 0:WM], wH[g][:].bitcast(F32), ALU.subtract
                                  ).then_inc(S("wsplit"), 1)

            def merge_chunk(i, last):
                for n in range(4):
                    for c in range(3):
                        j = 3 * n + c
                        dst = mT[:, bass.ds(i, 1), c * CH:(c + 1) * CH].rearrange("p a n -> p (a n)")
                        dve.wait_ge(S("sgd"), i * 12 + (j + 1))
                        dve.wait_ge(S("mb"), i * 12 + (j + 1))
                        bp = ps[:, (j % 2) * 2 + 1, 0:CH]
                        if n == 0:
                            dve.tensor_tensor(dst, sg[:, j % 2, :], bp, ALU.mult).then_inc(S("mp"), 1)
                        else:
                            dve.tensor_tensor(prod[:], sg[:, j % 2, :], bp, ALU.mult).then_inc(S("mp"), 1)
                            dve.wait_ge(S("mp"), i * 12 + (j + 3))
                            dve.tensor_tensor(dst, dst, prod[:], ALU.add).then_inc(S("macc"), 1)
                            dve.wait_ge(S("macc"), i * 9 + (j - 2))
                        if c == 1 and not (last and n == 3):
                            split_weights((n + 1) % 2, (i * 2 + ((n + 1) // 2 + 1)) * 16, i * 8 + (2 * n + 3))
                    dve.sem_inc(S("merge_free"), 1)

            split_weights(0, 16, 1)
            with dve.Fori(0, KD - 1) as i:
                merge_chunk(i, False)
            merge_chunk(KD - 1, True)
            dve.sem_inc(S("merged"), 1)
            dve.memset(ones2[:], 1.0)
            dve.memset(rv[:], 1.0)
            link(dve.memset(zid[:], 0))
            dve.sem_inc(S("zeroed"), 1)
            link(dve.memset(rt["s"][:], 0.0))
            dve.sem_inc(S("zeroed"), 1)
            dve.wait_ge(S("wo"), 80)
            for t in range(NT + 1):
                r = rows(t)
                dve.wait_ge(S(f"xin{t % 2}"), 16 * (t // 2 + 1))
                dve.wait_ge(S("y1"), t + 1)
                z = acc[0:r, t, :]
                for n in range(2):
                    m = dve.scalar_tensor_tensor(z[:, n * 512:(n + 1) * 512], xin[0:r, t % 2, n * 512:(n + 1) * 512], ALPHA,
                                                 ps[0:r, (t % 2) * 2 + n, :], ALU.mult, ALU.add)
                link(m)
                dve.sem_inc(S("z"), 1)
                norm_stats(dve, link, z, r, t)
                link(dve.tensor_scalar(z, z, mv2[0:r, 0:1], rv[0:r, 0:1], ALU.subtract, ALU.mult))
                link(dve.tensor_tensor(z, z, ln1[0][0:r, :], ALU.mult))
                dve.tensor_tensor(z, z, ln1[1][0:r, :], ALU.add).then_inc(S("x1"), 1)
            R = rt
            dve.wait_ge(S("rc"), 112)
            dve.wait_ge(S("score"), 1)
            link(dve.tensor_tensor(R["sel"][:], R["s"][:], R["brow"][:].rearrange("p (o e) -> p o e", o=1)
                                   .to_broadcast([P, 9, NE]), ALU.add))

            def ranks(v):
                link(dve.memset(cmp[:, 0:v.shape[1]], 0.0))
                for j in range(4):
                    n = v.shape[1]
                    if j < 3:
                        dve.tensor_tensor(cmp[:, 0:n, j + 1:4, j], v[:, :, j:j + 1].to_broadcast([P, n, 3 - j]),
                                          v[:, :, j + 1:4], ALU.is_ge)
                    if j > 0:
                        m = dve.tensor_tensor(cmp[:, 0:n, 0:j, j], v[:, :, j:j + 1].to_broadcast([P, n, j]),
                                              v[:, :, 0:j], ALU.is_gt)
                link(m)

            sel4 = R["sel"][:].rearrange("p t (g e) -> p (t g) e", g=4)
            cho4 = R["chosen"][:].rearrange("p t (g e) -> p (t g) e", g=4)
            ranks(sel4)
            link(dve.tensor_reduce(cho4, cmp[:], AX.X, ALU.add))
            link(dve.tensor_scalar(cho4, cho4, 1.5, None, ALU.is_lt))
            link(dve.tensor_tensor(R["tmp"][:], R["sel"][:], R["chosen"][:], ALU.mult))
            link(dve.tensor_reduce(R["gsc"][:].rearrange("p t g -> p (t g)"),
                                   R["tmp"][:].rearrange("p t (g e) -> p (t g) e", g=4), AX.X, ALU.add))
            ranks(R["gsc"][:])
            link(dve.tensor_reduce(R["gin"][:], cmp[:, 0:9], AX.X, ALU.add))
            link(dve.tensor_scalar(R["gin"][:], R["gin"][:], 0.5, None, ALU.is_lt))
            link(dve.tensor_tensor(R["gin"][:], R["gin"][:], valid[:].rearrange("p (t o) -> p t o", o=1)
                                   .to_broadcast([P, 9, 4]), ALU.mult))
            dve.tensor_tensor(cho4, cho4, R["gin"][:].rearrange("p t g -> p (t g)").rearrange("p (n o) -> p n o", o=1)
                              .to_broadcast([P, 36, 4]), ALU.mult).then_inc(S("mask"), 1)
            dve.wait_ge(S("mask"), 1)
            link(dve.tensor_tensor(R["gate"][:], R["s"][:], R["chosen"][:], ALU.mult))
            link(dve.tensor_reduce(R["gsum"][:], R["gate"][:], AX.X, ALU.add))
            link(dve.tensor_scalar(R["gsum"][:], R["gsum"][:], 1e-30, None, ALU.max))
            link(dve.reciprocal(R["gsum"][:], R["gsum"][:]))
            link(dve.tensor_tensor(R["gate"][:], R["gate"][:], R["gsum"][:].rearrange("p (t o) -> p t o", o=1)
                                   .to_broadcast([P, 9, NE]), ALU.mult))
            dve.wait_ge(S("pos"), 1)
            tot = ps[:, 7, 256:400].rearrange("p (t e) -> p t e", e=NE)
            link(dve.memset(R["pre"][:, 0, :], 0.0))
            for t in range(1, 9):
                link(dve.tensor_tensor(R["pre"][:, t, :], R["pre"][:, t - 1, :], tot[:, t - 1, :], ALU.add))
            link(dve.tensor_tensor(R["ne"][:], R["pre"][:, 8, :], tot[:, 8, :], ALU.add))
            link(dve.tensor_scalar(R["nt"][:], R["ne"][:], 0.5, None, ALU.is_gt))
            for m in range(1, 9):
                link(dve.scalar_tensor_tensor(R["nt"][:], R["ne"][:], m * P + 0.5, R["nt"][:], ALU.is_gt, ALU.add))
            link(dve.tensor_copy(R["inc"][:, 0, :], R["nt"][:]))
            cur = 0
            for d in (1, 2, 4, 8):
                dve.tensor_copy(R["inc"][:, 1 - cur, 0:d], R["inc"][:, cur, 0:d])
                link(dve.tensor_tensor(R["inc"][:, 1 - cur, d:16], R["inc"][:, cur, d:16], R["inc"][:, cur, 0:16 - d], ALU.add))
                cur = 1 - cur
            inc = R["inc"][:, 0, :]
            link(dve.tensor_tensor(R["ne"][:], inc, R["nt"][:], ALU.subtract))
            link(dve.tensor_tensor(R["pos"][:], ps[:, 7, 0:144].rearrange("p (t e) -> p t e", e=NE), R["pre"][:], ALU.add))
            link(dve.scalar_tensor_tensor(R["pos"][:], R["ne"][:].rearrange("p (o e) -> p o e", o=1).to_broadcast([P, 9, NE]),
                                          float(P), R["pos"][:], ALU.mult, ALU.add))
            link(dve.tensor_tensor(R["pos"][:], R["pos"][:], R["chosen"][:], ALU.mult))
            link(dve.tensor_reduce(R["slotf"][:, 1, :], R["pos"][:], AX.X, ALU.max))
            link(dve.tensor_scalar(R["tmp"][:], R["chosen"][:], -1e6, 1e6, ALU.mult, ALU.add))
            link(dve.tensor_tensor(R["tmp"][:], R["tmp"][:], R["pos"][:], ALU.add))
            link(dve.tensor_reduce(R["slotf"][:, 0, :], R["tmp"][:], AX.X, ALU.min))
            for c in range(2):
                sl = R["slotf"][:, c, :].rearrange("p (t o) -> p t o", o=1).to_broadcast([P, 9, NE])
                link(dve.tensor_tensor(R["pre"][:], R["tmp"][:], sl, ALU.is_equal))
                link(dve.tensor_tensor(R["pre"][:], R["pre"][:], R["gate"][:], ALU.mult))
                link(dve.tensor_reduce(R["gw"][:, :, c], R["pre"][:], AX.X, ALU.add))
                link(dve.tensor_copy(R["slot"][:, :, c], R["slotf"][:, c, :]))
            link(dve.tensor_tensor(cmp32[:], inc.rearrange("p (o e) -> p o e", o=1).to_broadcast([P, 32, NE]),
                                   tileno[:].rearrange("p (n o) -> p n o", o=1).to_broadcast([P, 32, NE]), ALU.is_le))
            link(dve.tensor_reduce(R["te"][:], cmp32[:], AX.X, ALU.add))
            link(dve.tensor_scalar(R["te"][:], R["te"][:], float(NE - 1), None, ALU.min))
            link(dve.tensor_copy(R["tei"][:], R["te"][:]))
            for nm in ("w13_free", "w2_free"):
                dve.sem_inc(S(nm), 2)
            for nm in ("ys0", "ys1"):
                dve.sem_inc(S(nm), 16)
            for nm in ("xga_free", "xgb_free", "ya", "yb", "hT"):
                dve.sem_inc(S(nm), 1)
            dve.sem_inc(S("h_free"), 2)
            dve.sem_inc(S("xg_free"), 2)
            dve.sem_inc(S("routed"), 1)

            def rows_T(u, n):
                dve.wait_ge(S("xtrb"), n[0])
                dve.tensor_copy(xgT[:, u, 4:8, :].rearrange("p k r -> p (k r)"), ps[:, 5, :]).then_inc(S("xgb"), 1)
                dve.wait_ge(S("xgb"), n[0])
                dve.sem_inc(S("xgb_free"), 1)
                dve.sem_inc(S("xg_free"), 1)

            def times(u, n):
                dve.wait_ge(S("hs"), n[0])
                dve.tensor_tensor(hn[:, u, :], hs[:, u, :], ps[:, u, FE:2 * FE], ALU.mult).then_inc(S("h"), 1)
                dve.wait_ge(S("h"), n[0])
                dve.sem_inc(S("h_free"), 1)
                dve.sem_inc(S("w13_free"), 1)

            def hidden_T(u, n):
                dve.wait_ge(S("htr"), n[0])
                dve.tensor_copy(hT[:, u].rearrange("p f r -> p (f r)"), ps[:, 6, 0:2 * P]).then_inc(S("hT"), 1)

            def out_b(u, n):
                dve.wait_ge(S("dnb"), n[0])
                dve.wait_ge(S(f"ys{u}"), n[1])
                dve.tensor_copy(yo[:, u, 512:D], ps[:, 3, :]).then_inc(S("yb"), 1)
                dve.sem_inc(S("w2_free"), 1)

            def vals(i, k):
                T = i * 2 + k
                return (T + 1, (i + k // 2) * 16 + 16)

            rows_T(0, vals(0, 0))
            rows_T(1, vals(0, 1))
            times(0, vals(0, 0))
            with dve.Fori(0, MOE_TILES // 2 - 1) as i:
                for u in range(2):
                    times(1 - u, vals(i, u + 1))
                    hidden_T(u, vals(i, u))
                    rows_T(u, vals(i, u + 2))
                    out_b(u, vals(i, u))
            i = MOE_TILES // 2 - 1
            times(1, vals(i, 1))
            hidden_T(0, vals(i, 0))
            out_b(0, vals(i, 0))
            hidden_T(1, vals(i, 1))
            out_b(1, vals(i, 1))
            dve.wait_ge(S("acc_act"), NT + 1)
            def combine(t):
                r = rows(t)
                z = acc[0:r, t, :]
                f = fs[0:r, t % 4]
                dve.wait_ge(S(f"yg{t % 4}"), 32 * (t // 4 + 1))
                for c in range(2):
                    link(dve.scalar_tensor_tensor(z, yg[0:r, t % 4, c, :], rt["gw"][0:r, t, c:c + 1], z, ALU.mult, ALU.add))
                dve.sem_inc(S("yg_free"), 1)
                for c in range(2):
                    m = dve.bn_stats(st12[0:r, c, :], z[:, c * 512:(c + 1) * 512])
                link(m)
                link(dve.bn_aggr(f[:, 0:2], st12[0:r].rearrange("p c s -> p (c s)")))
                dve.tensor_scalar(f[:, 2:3], f[:, 1:2], EPS, None, ALU.add).then_inc(S("var"), 1)

            def scale(t):
                f = fs[0:rows(t), t % 4]
                dve.wait_ge(S("sd"), NT + 1 + t + 2)
                link(dve.reciprocal(f[:, 4:5], f[:, 3:4]))
                dve.scalar_tensor_tensor(f[:, 5:6], f[:, 0:1], -1.0, f[:, 4:5], ALU.mult, ALU.mult).then_inc(S("fsd"), 1)

            def gain(t):
                r = rows(t)
                z = acc[0:r, t, :]
                dve.wait_ge(S("acc_act"), NT + 1 + t + 1)
                link(dve.tensor_tensor(z, z, ln2[0:r, 0, :], ALU.mult))
                dve.tensor_tensor(z, z, ln2[0:r, 1, :], ALU.add).then_inc(S("y_ready"), 1)

            for t in range(NT + 3):
                if t <= NT:
                    combine(t)
                if 1 <= t <= NT + 1:
                    scale(t - 1)
                if t >= 2:
                    gain(t - 2)

        def emit_pool2(pool):
            pool.wait_ge(S("routed"), 1)
            pool.wait_ge(S("ids0"), 16)
            for t in range(NT + 1):
                r = rows(t)
                for c in range(2):
                    pool.indirect_dma_start(a["ids"], bass.IndirectOffsetOnAxis(rt["slot"][0:r, t, c:c + 1], 0),
                                            tok[0:r, t:t + 1], None).then_inc(S("scat"), 16)
            pool.wait_ge(S("scat"), 16 * 2 * (NT + 1))
            pool.dma_start(idall[:], a["ids"].rearrange("(n p) o -> p (n o)", p=P), allow_slow_non_contiguous=True).then_inc(S("idall"), 16)
            pool.wait_ge(S("idall"), 16)
            with pool.Fori(0, MOE_TILES // 2) as i:
                for u in range(2):
                    v = pool.snap(i * 2 + (u + 1), min_val=1, max_val=MOE_TILES)
                    src = idall[:, bass.ds(i * 2 + u, 1)]
                    pool.wait_ge(S("xg_free"), v)
                    pool.wait_ge(S("idall"), 16)
                    pool.tensor_copy(idt[:, u:u + 1], src).then_inc(S("idt"), 1)
                    pool.wait_ge(S("x1d"), 16 * (NT + 1))
                    pool.wait_ge(S("idt"), v)
                    pool.indirect_dma_start(xg[:, u, :], None, a["x1"],
                                            bass.IndirectOffsetOnAxis(idt[:, u:u + 1], 0)).then_inc(S(f"xg{u}"), 16)
            for t in range(NT + 1):
                r = rows(t)
                if t == 0:
                    pool.wait_ge(S("ys0"), 16 * (MOE_TILES // 2 + 1))
                    pool.wait_ge(S("ys1"), 16 * (MOE_TILES // 2 + 1))
                if t >= 4:
                    pool.wait_ge(S("yg_free"), t - 3)
                for c in range(2):
                    pool.indirect_dma_start(yg[0:r, t % 4, c, :], None, a["yd"],
                                            bass.IndirectOffsetOnAxis(rt["slot"][0:r, t, c:c + 1], 0)).then_inc(S(f"yg{t % 4}"), 16)

        block = ctx.enter_context(nc.Block())

        @block.sync
        def _(sp):
            sp.dma_start(ident[:], a["ident"]).then_inc(S("ident"), 16)

            def load_w(n):
                c0, cw = CHUNKS[ORDER[n]]
                if n >= 2:
                    sp.wait_ge(S("proj"), 9 * (n - 1))
                for kh in range(2):
                    sp.dma_start(w_ring[:, n % 2, kh * 4:kh * 4 + 4, 0:cw],
                                 a["w_in"][:, kh * 4:kh * 4 + 4, c0:c0 + cw]).then_inc(S(f"w{n % 2}"), 16)

            sp.dma_start(xT[:, :, SEQ:TOK], a["xT"][:, :, SEQ:TOK]).then_inc(S("xs"), 16)
            load_w(0)
            for q in range(4):
                sp.dma_start(xT[:, :, q * 256:q * 256 + 256],
                             a["xT"][:, :, q * 256:q * 256 + 256]).then_inc(S(f"xq{q}"), 16)
            load_w(1)
            sp.dma_start(t5[0:NBUCK, :], a["t5_table"]).then_inc(S("tbl"), 16)
            sp.dma_start(oh_rev[:], a["oh_rev"]).then_inc(S("tbl"), 16)
            sp.dma_start(oh_dec[:], a["oh_dec"]).then_inc(S("tbl"), 16)
            sp.dma_start(bfb[:], a["b_forget"].to_broadcast([P, H])).then_inc(S("cst"), 16)
            sp.dma_start(tri_neg[:], a["tri_neg"]).then_inc(S("cst"), 16)
            sp.dma_start(trisA[:], a["tri_after"]).then_inc(S("cst"), 16)
            sp.dma_start(causal[:], a["causal"]).then_inc(S("cst"), 16)
            sp.dma_start(gbB[:, 0, :], a["sgu_ln_g"].to_broadcast([P, W])).then_inc(S("cst"), 16)
            sp.dma_start(gbB[:, 1, :], a["sgu_ln_b"].to_broadcast([P, W])).then_inc(S("cst"), 16)
            sp.dma_start(wsp[:], a["w_spatial"]).then_inc(S("cst"), 16)
            sp.dma_start(trilB[:], a["tril_T"]).then_inc(S("cst"), 16)
            sp.dma_start(bsp[:], a["b_spatial"]).then_inc(S("cst"), 16)
            sp.dma_start(swb[0:NB, 0, :], a["w_spatial_00"].to_broadcast([NB, 4])).then_inc(S("cst"), 16)
            sp.dma_start(swb[0:NB, 1, :], a["b_spatial_0"].to_broadcast([NB, 4])).then_inc(S("cst"), 16)
            sp.dma_start(bNew[:], a["new_mask"]).then_inc(S("cst"), 16)
            sp.dma_start(ptk[:], a["row_group"]).then_inc(S("cst"), 16)
            sp.dma_start(psc[:], a["pool_scale"]).then_inc(S("cst"), 16)
            for b in range(NB):
                sp.dma_start(ptb[:, b:b + 1], a["page_rep"][b].rearrange("(p o) -> p o", o=1)).then_inc(S("cst"), 16)
            sp.wait_ge(S("tb_src"), 12)
            sp.dma_start(a["tb_dram"].rearrange("h (p u) -> p h u", p=P), tb_src[:]).then_inc(S("tb_out"), 16)
            load_w(2)

            def store_nat(chunk, kcol, out, src_out):
                for t in TILE_ORDER[1:]:
                    sp.wait_ge(S("evicted"), pj_index(chunk, t) + 1)
                    sp.dma_start(a[out][t * P:(t + 1) * P, :],
                                 nat[:, t % 2, kcol:kcol + W]).then_inc(S(f"st{t % 2}"), 16)

            def sample_out(chunk, pieces):
                c0, cw = SC[chunk], CHUNKS[chunk][1]
                sp.wait_ge(S("evicted"), pj_index(chunk, NT) + 1)
                sp.dma_start(a["s_dram"][:, c0:c0 + cw], s_nat[0:NB, c0:c0 + cw]).then_inc(S(f"sd_{chunk}"), 16)
                for out, lo in pieces:
                    sp.dma_start(a[out], s_nat[0:NB, lo:lo + W]).then_inc(S("out"), 16)

            sp.wait_ge(S("v_done"), 1)
            sp.dma_start(a["vb_s"], uv[0:NB, NT, W:2 * W]).then_inc(S("out_vb"), 16)
            sample_out("qka", [("k_a_s", 256)])
            store_nat("qka", W, "k_a_p", None)
            load_w(3)
            sample_out("vfa", [("v_a_s", 512)])
            sp.wait_ge(S("evicted"), pj_index("vfa", NT - 1) + 1)
            sp.dma_start(a["v_a_p"].rearrange("(t p) w -> p t w", p=P), va[:]).then_inc(S("out_va"), 16)
            sp.wait_ge(S("lf"), 1)
            sp.dma_start(a["lf_p"].rearrange("(t p) h -> p t h", p=P), lf[:, 0:NT, :]).then_inc(S("out_lf"), 16)
            sp.dma_start(a["lf_s"], lf[0:NB, NT, :]).then_inc(S("out_lf"), 16)
            sp.wait_ge(S("out_lf"), 32)
            sp.dma_start(lgb[:], a["lf_s"].rearrange("b h -> (b h)").rearrange("(o n) -> o n", o=1)
                         .to_broadcast([P, 32])).then_inc(S("lgb"), 16)
            load_w(4)
            sp.wait_ge(S("tb_out"), 16)
            sp.wait_ge(S("pt_free0"), OUT_DONE[0])
            sp.dma_start(bands[:], a["bands"]).then_inc(S("bands"), 16)
            sp.wait_ge(S("wpb0"), 1)
            for g in range(4):
                lo = 64 * (g % 2)
                sp.dma_start(wpb[lo:lo + 64, g // 2, lo:lo + 64], a["w_pool"][g]).then_inc(S("bands"), 16)
            sample_out("qkc", [("k_c_s", 1028)])
            store_nat("qkc", W, "k_c_p", None)
            sample_out("vpd", [("v_c_s", 1284), ("pd_s", 1540)])
            sp.wait_ge(S("proj"), 36)
            sp.dma_start(spool[0:NB, 0:15, :], a["state_pool"]).then_inc(S("spool"), 16)
            sp.dma_start(spool[0:NB, 15, :], s_nat[0:NB, 1540:1796]).then_inc(S("spool"), 16)
            sp.wait_ge(S("evicted"), pj_index("vpd", NT - 1) + 1)
            sp.dma_start(a["v_c_p"].rearrange("(t p) w -> p t w", p=P), vp[:, :, 0:W]).then_inc(S("out_vc"), 16)
            sp.dma_start(a["pool_p"], vp[P - 15:P, NT - 1, W:2 * W]).then_inc(S("out_pool"), 16)
            sp.wait_ge(S("oD"), 1)
            for h in range(H):
                src = a["tb_dram"][h, P - 1:P - 1 + P * (TBW - 1)].rearrange("(p u) -> p u", u=TBW - 1)[:, 0:SEQ]
                sp.dma_start(tb[:, h, :], src).then_inc(S("tb_in"), 16)
            emit_sp2(sp)

        @block.tensor
        def _(pe):
            mm = nc.tensor.matmul

            def tr(out, in_, n=P):
                return nc.tensor.transpose(out, in_, ident[0:n, 0:n])

            def project(chunk, t):
                n = ORDER.index(chunk)
                cw = CHUNKS[chunk][1]
                j = pj_index(chunk, t)
                pe.wait_ge(S(f"w{n % 2}"), 32 * (n // 2 + 1))
                if n == 0:
                    pe.wait_ge(S("xs") if t == NT else S(f"xq{t // 2}"), 16)
                if j >= 2:
                    pe.wait_ge(S("evicted"), j - 1)
                r = rows(t)
                for k in range(KD):
                    m = mm(ps[0:r, j % 2, 0:cw], xT[:, k, t * P:t * P + r], w_ring[:, n % 2, k, 0:cw],
                           start=(k == 0), stop=(k == KD - 1))
                m.then_inc(S("proj"), 1)

            pe.wait_ge(S("tbl"), 48)
            pe.wait_ge(S("cleared"), 1)
            for h in range(H):
                for q in range(3):
                    n = h * 3 + q
                    if n >= 2:
                        pe.wait_ge(S("tb_src"), n - 1)
                    mm(ps[:, 6 + n % 2, 0:384], t5[:, h:h + 1].to_broadcast([NBUCK + 1, P]), oh_rev[:, q * 384:(q + 1) * 384],
                       start=True, stop=True).then_inc(S("tb_mm"), 1)
            pe.wait_ge(S("tb_src"), 12)
            for i in range(4):
                m = mm(ps[:, 6, i * H:(i + 1) * H], oh_dec[:, i, :], t5[:], start=True, stop=True)
            m.then_inc(S("tb_mm"), 1)

            for t in TILE_ORDER:
                project("uv", t)
            pe.wait_ge(S("wsp_m"), 4)
            pe.wait_ge(S("v_done"), 1)
            for g in range(4):
                if g >= 2:
                    pe.wait_ge(S("ob"), g - 1)
                elif g == 0:
                    pe.wait_ge(S("tb_src"), 13)
                mm(ps[:, 6 + g % 2, :].rearrange("p (t c) -> p t c", t=NT), wsp[:, g, :],
                   uv[:, 0:NT, W + 64 * g:W + 64 * g + 64], start=True, stop=True).then_inc(S("band_mm"), 1)
            pe.wait_ge(S("ob"), 5)
            for t in range(NT + 1):
                if t >= 2:
                    pe.wait_ge(S("obT"), t - 1)
                r = rows(t)
                for f in range(2):
                    m = tr(ps[:, 4 + t % 2, f * P:f * P + r], uv[0:r, t, f * P:(f + 1) * P], r)
                m.then_inc(S("ob_tr"), 1)

            def qk_transposes(chunk, t, base):
                i = TILE_ORDER.index(t)
                pe.wait_ge(S("evicted"), pj_index(chunk, t) + 1)
                if i >= 3:
                    pe.wait_ge(S(f"qkT_{chunk}"), i - 2)
                elif chunk == "qka":
                    pe.wait_ge(S("obT"), NT + 1)
                else:
                    pe.wait_ge(S("pt_free0"), PTC[0])
                    pe.wait_ge(S("pt_free1"), PTC[1])
                for f in range(4):
                    m = tr(ps[:, 4 + t % 2, f * P:(f + 1) * P], nat[:, t % 2, f * P:(f + 1) * P])
                m.then_inc(S(f"qk_tr_{chunk}"), 1)

            for i, t in enumerate(TILE_ORDER):
                project("qka", t)
                if i >= 2:
                    qk_transposes("qka", TILE_ORDER[i - 1], 0)
            qk_transposes("qka", 7, 0)
            for t in TILE_ORDER:
                project("vfa", t)
            pe.wait_ge(S("lf"), 1)
            pe.wait_ge(S("lpre"), 1)
            n = 0
            for h in range(H):
                for half in range(2):
                    if n >= 2:
                        pe.wait_ge(S("fb"), n - 1)
                    elif n == 0:
                        pe.wait_ge(S("ob"), 5)
                    for q in range(4):
                        t = half * 4 + q
                        o_ = ps[:, 6 + n % 2, q * P:(q + 1) * P]
                        mm(o_, lf[:, t, h:h + 1].to_broadcast([P, P]), tri_neg[:], start=True, stop=(t == 0))
                        if t:
                            m = mm(o_, lpre[:, t, h:h + 1].to_broadcast([P, P]), ones_neg[:], start=False, stop=True)
                    m.then_inc(S("fb_mm"), 1)
                    n += 1

            def attention(br, bias_ready, v_of):
                def scores(n):
                    qt, h = items[n]
                    L = P * (qt + 1)
                    if n >= 2:
                        pe.wait_ge(S("sc_free"), 32 * br + n - 1)
                    lo = 64 * (h % 2)
                    for c in range(0, L, 512):
                        e = min(L, c + 512)
                        last = e == L and br == 0
                        m = mm(ps[:, 2 * (n % 2) + c // 512, 0:e - c], qT[lo:lo + 64, h // 2, qt * P:(qt + 1) * P],
                               kT[lo:lo + 64, h // 2, c:e], start=True, stop=not last)
                        if last:
                            m = mm(ps[:, 2 * (n % 2) + c // 512, e - c - P:e - c], ident[:], causal[:],
                                   start=False, stop=True)
                    m.then_inc(S("sc"), 1)

                def transposes(n):
                    qt, h = items[n]
                    pe.wait_ge(S("ex"), 32 * br + n + 1)
                    for c in range(1 + (qt >= 4)):
                        pe.wait_ge(S(f"pt_free{c}"), PT_USES[br][n][c])
                        for k in range(4 * c, min(qt + 1, 4 * c + 4)):
                            m = tr(ps[:, 4 + c, (k % 4) * P:(k % 4 + 1) * P], p_sb[:, n % 2, k * P:(k + 1) * P])
                        m.then_inc(S(f"pt{c}"), 1)

                def values(n):
                    qt, h = items[n]
                    if n >= 2:
                        pe.wait_ge(S("on"), 32 * br + n - 1)
                    for c in range(1 + (qt >= 4)):
                        pe.wait_ge(S(f"pt_free{c}"), PT_USES[br][n][c] + 1)
                        for k in range(4 * c, min(qt + 1, 4 * c + 4)):
                            m = mm(ps[:, 6 + n % 2, 0:64], p_T[:, n % 2, k * P:(k + 1) * P], v_of(k, h),
                                   start=(k == 0), stop=(k == qt))
                    m.then_inc(S("pv"), 1)

                def out_transposes(qt):
                    pe.wait_ge(S("on"), 32 * br + 4 * qt + 4)
                    pe.wait_ge(S("pt_free0"), OUT_USES[br][qt])
                    for f in range(2):
                        m = tr(ps[:, 4, f * P:(f + 1) * P], o_nat[:, qt % 2, f * P:(f + 1) * P])
                    m.then_inc(S("ot"), 1)

                bias_ready()
                scores(0)
                scores(1)
                for n in range(32):
                    transposes(n)
                    if n + 2 < 32:
                        scores(n + 2)
                    values(n)
                    if items[n][1] == 1 and items[n][0] > 0:
                        out_transposes(items[n][0] - 1)
                out_transposes(NT - 1)

            def bias_a():
                pe.wait_ge(S("fb"), 8)
                pe.wait_ge(S("evicted"), 27)
                pe.wait_ge(S("qkT_qka"), 8)

            attention(0, bias_a, lambda k, h: va[:, k, h * 64:h * 64 + 64])
            def softmax_steps(br, end):
                def top():
                    pe.wait_ge(S("dmx"), br + 1)
                    tr(ps[:, 6, 0:P], mx[:]).then_inc(S("dmx_tr"), 1)

                def spread():
                    pe.wait_ge(S("dmc"), br + 1)
                    mm(ps[:, 6, P:P + 32], mcol[0:32, 0:1].to_broadcast([32, P]), ident[0:32, 0:32],
                       start=True, stop=True).then_inc(S("dmb"), 1)

                def total():
                    pe.wait_ge(S("dsum"), br + 1)
                    mm(ps[:, 6, 2 * P:2 * P + 32], ones[:], dsum[:], start=True, stop=True).then_inc(S("dtot"), 1)

                return [top, spread, total]

            def values_a(s):
                b, half = s // 2, s % 2
                pe.wait_ge(S("dp"), 1)
                pe.wait_ge(S(f"vdma{s % 2}"), VD_A[s])
                nr = 8 + half
                for f in range(2):
                    for r in range(nr):
                        m = mm(ps[:, 6 + f, 2 * b:2 * b + 2], kv[:, s % 2, r, f * P:(f + 1) * P],
                               sA[:, b, half * 8 + r, 2 * f:2 * f + 2],
                               start=(r == 0 and half == 0), stop=(r == nr - 1 and half == 1))
                m.then_inc(S("dv"), 1)

            pe.wait_ge(S("ltot"), 1)
            pe.wait_ge(S("on"), 32)
            mm(ps[:, 6, 0:32], trisA[:], ltot[:], start=True, stop=True).then_inc(S("lsuf"), 1)
            pe.wait_ge(S("pt_free0"), OUT_DONE[0])
            between = softmax_steps(0, 1) + [lambda s=s: values_a(s) for s in range(16)]
            pe.wait_ge(S("sc_free"), 32)
            for i, t in enumerate(TILE_ORDER):
                project("qkc", t)
                if i >= 2:
                    qk_transposes("qkc", TILE_ORDER[i - 1], 0)
                between.pop(0)()
            qk_transposes("qkc", 7, 0)
            for t in TILE_ORDER:
                project("vpd", t)
                between.pop(0)()
            while between:
                between.pop(0)()
            pe.wait_ge(S("bands"), 80)
            pe.wait_ge(S("evicted"), 45)
            for g in range(4):
                if g >= 2:
                    pe.wait_ge(S("dn"), g - 1)
                col = slice(W + 64 * g, W + 64 * g + 64)
                pg = ps[:, g % 2, :].rearrange("p (t c) -> p t c", t=NT)
                mm(pg[:, 1:NT, :], bands[:, g, 1, :], vp[:, 1:NT, col], start=True, stop=False)
                mm(pg[:, 1:NT, :], bands[:, g, 2, :], vp[:, 0:NT - 1, col], start=False, stop=True)
                mm(pg[:, 0, :], bands[:, g, 0, :], vp[:, 0, col], start=True, stop=True).then_inc(S("band_mm"), 1)
            pe.wait_ge(S("dn"), 5)
            for t in range(NT + 1):
                if t >= 2:
                    pe.wait_ge(S("dT"), t - 1)
                else:
                    pe.wait_ge(S("qkT_qkc"), 8)
                r = rows(t)
                src = vp[:, t, W:2 * W] if t < NT else sd[0:NB, :]
                for f in range(2):
                    m = tr(ps[:, 4 + t % 2, f * P:f * P + r], src[:, f * P:(f + 1) * P], r)
                m.then_inc(S("d_tr"), 1)
            pe.wait_ge(S("dT"), NT + 1)
            for f in range(2):
                for c in range(3):
                    n = f * 3 + c
                    if n >= 2:
                        pe.wait_ge(S("oDn"), n - 1)
                    mm(ps[:, n % 2, 0:CH], wpb[:, f, :], dT[:, f, c * CH:(c + 1) * CH],
                       start=True, stop=True).then_inc(S("po_mm"), 1)

            def bias_c():
                pe.wait_ge(S("tb_in"), 64)
                pe.wait_ge(S("oDn"), 6)
                pe.wait_ge(S("so"), 1)

            attention(1, bias_c, lambda k, h: vp[:, k, h * 64:h * 64 + 64])
            pe.wait_ge(S("on"), 64)
            pe.wait_ge(S("pt_free0"), OUT_DONE[1])
            pe.sem_inc(S("merge_free"), 2)
            for step in softmax_steps(1, 0):
                step()
            pe.wait_ge(S("dp"), 2)
            for b in range(NB):
                pe.wait_ge(S(f"vdma{b % 2}"), VD_C[b])
                for f in range(2):
                    for r in range(4):
                        m = mm(ps[:, 6 + f, 2 * b:2 * b + 2], kv[:, b % 2, 5 + r, f * P:(f + 1) * P],
                               sC[:, b, r, 2 * f:2 * f + 2], start=(r == 0), stop=(r == 3))
                m.then_inc(S("dv"), 1)
            emit_pe2(pe, mm, tr)

        @block.scalar
        def _(act):
            def evict(chunk, t):
                j = pj_index(chunk, t)
                act.wait_ge(S("proj"), j + 1)
                r = rows(t)
                src = ps[0:r, j % 2, :]
                if chunk == "uv":
                    act.activation(uv[0:r, t, :], src, ACT.Gelu_apprx_tanh).then_inc(S("evicted"), 1)
                    return
                if t == NT:
                    cw = CHUNKS[chunk][1]
                    if chunk == "vfa":
                        act.wait_ge(S("cleared"), 2)
                        act.copy(fa[0:r, NT, :], src[:, W:W + H])
                    act.copy(s_nat[0:r, SC[chunk]:SC[chunk] + cw], src[:, 0:cw]).then_inc(S("evicted"), 1)
                    return
                i = TILE_ORDER.index(t)
                if chunk in ("qka", "qkc"):
                    if i >= 3:
                        act.wait_ge(S(f"qk_tr_{chunk}"), i - 2)
                        act.wait_ge(S(f"st{t % 2}"), 16 * (t // 2 + 4 * (chunk == "qkc")))
                    elif chunk == "qkc":
                        act.wait_ge(S("ot"), NT)
                    act.copy(nat[:, t % 2, :], src).then_inc(S("evicted"), 1)
                elif chunk == "vfa":
                    if i == 1:
                        act.wait_ge(S("obT"), NT + 1)
                        act.wait_ge(S("out_vb"), 16)
                    act.copy(va[:, t, :], src[:, 0:W])
                    act.copy(fa[:, t, :], src[:, W:W + H]).then_inc(S("evicted"), 1)
                else:
                    if i == 1:
                        act.wait_ge(S("pv"), 32)
                        act.wait_ge(S("out_va"), 16)
                    act.copy(vp[:, t, :], src).then_inc(S("evicted"), 1)

            for t in TILE_ORDER:
                evict("uv", t)
            act.wait_ge(S("var"), 1)
            act.activation(rs[:], rs2[:], ACT.Sqrt).then_inc(S("sd"), 1)
            for t in TILE_ORDER:
                evict("qka", t)
            for t in TILE_ORDER:
                evict("vfa", t)
            act.wait_ge(S("faz"), 1)
            act.activation(fae[:], faz[:], ACT.Exp, scale=-1.0).then_inc(S("softplus"), 1)
            act.wait_ge(S("softplus"), 1)
            act.activation(fal[:], fae[:], ACT.Ln, bias=1.0).then_inc(S("softplus"), 1)

            def attention(br):
                def weights(n):
                    qt, h = items[n]
                    L = P * (qt + 1)
                    act.wait_ge(S("sc_free"), 32 * br + n + 1)
                    act.activation(p_sb[:, n % 2, 0:L], p_sb[:, n % 2, 0:L], ACT.Exp, scale=-1.0,
                                   bias=am[:, n % 4:n % 4 + 1],
                                   accum_out=asum[:, n % 4:n % 4 + 1]).then_inc(S("ex"), 1)

                def blocks(n):
                    qt, h = items[n]
                    w = min(512, P * (qt + 1))
                    act.wait_ge(S("pt0"), 32 * br + n + 1)
                    if n >= 2:
                        act.wait_ge(S("pv"), 32 * br + n - 1)
                    act.copy(p_T[:, n % 2, 0:w], ps[:, 4, 0:w]).then_inc(S("pt_free0"), 1)

                def out_T(qt):
                    act.wait_ge(S("ot"), NT * br + qt + 1)
                    act.copy(oT[:, 2 * br, :, qt * P:(qt + 1) * P],
                             ps[:, 4, 0:2 * P].rearrange("p (f r) -> p f r", f=2)).then_inc(S("pt_free0"), 1)

                weights(0)
                weights(1)
                for n in range(32):
                    blocks(n)
                    if n + 2 < 32:
                        weights(n + 2)
                    if items[n][1] == 1 and items[n][0] > 0:
                        out_T(items[n][0] - 1)
                out_T(NT - 1)

            attention(0)
            for i, t in enumerate(TILE_ORDER):
                if i == 2:
                    act.wait_ge(S("dsh"), 1)
                    act.activation(sA[:], sA[:], ACT.Exp).then_inc(S("dex"), 1)
                evict("qkc", t)
            for t in TILE_ORDER:
                evict("vpd", t)
            for n in range(6):
                f, c = n // 3, n % 3
                act.wait_ge(S("po_mm"), n + 1)
                act.activation(oT[:, 3, f, c * CH:(c + 1) * CH], ps[:, n % 2, 0:CH], ACT.Copy,
                               scale=psc[:, f:f + 1]).then_inc(S("oDn"), 1)
            act.wait_ge(S("oDn"), 6)
            act.sem_inc(S("oD"), 1)
            attention(1)
            act.wait_ge(S("dsh"), 2)
            act.activation(sC[:], sC[:], ACT.Exp).then_inc(S("dex"), 1)
            emit_act2(act)

        @block.vector
        def _(dve):
            n_chain = [0]

            def link(ins):
                n_chain[0] += 1
                ins.then_inc(S("dve_chain"), 1)
                dve.wait_ge(S("dve_chain"), n_chain[0])

            link(dve.memset(t5[NBUCK:NBUCK + 1, :], 1.0))
            dve.sem_inc(S("cleared"), 1)
            link(dve.memset(fa[:], 0.0))
            dve.sem_inc(S("cleared"), 1)
            dve.memset(ones[:], 1.0)
            dve.memset(ones_neg[:], -1.0)
            dve.memset(mx[:], 0.0)
            link(dve.memset(kv[:, :, 8, :], 0.0))
            dve.sem_inc(S("cleared"), 1)
            dve.wait_ge(S("tbl"), 48)
            for n in range(12):
                h, q = n // 3, n % 3
                dve.wait_ge(S("tb_mm"), n + 1)
                dve.tensor_copy(tb_src[:, h, q * 384:(q + 1) * 384], ps[:, 6 + n % 2, 0:384]).then_inc(S("tb_src"), 1)
            dve.wait_ge(S("tb_mm"), 13)
            dve.tensor_copy(bC[:].rearrange("p s h -> p (s h)"), ps[:, 6, 0:16]).then_inc(S("tb_src"), 1)
            dve.wait_ge(S("cst"), 16 * 22)
            for c, mul in ((0, 16.0), (1, 16.0), (2, 8.0)):
                m = dve.tensor_scalar(idx[:, :, c], ptb[:], mul, ptk[:, c:c + 1], ALU.mult, ALU.add)
            link(m)
            dve.sem_inc(S("idx"), 1)
            for g in range(4):
                dve.tensor_tensor(wsp[:, g, :], wsp[:, g, :], trilB[:], ALU.mult).then_inc(S("wsp_m"), 1)
            for i, t in enumerate(TILE_ORDER):
                r = rows(t)
                dve.wait_ge(S("evicted"), i + 1)
                if i == 0:
                    link(dve.memset(mv[:], 1.0))
                link(dve.bn_stats(st6[0:r, 0, :], uv[0:r, t, W:2 * W]))
                link(dve.bn_aggr(mv[0:r, t, :], st6[0:r, 0, :]))
            dve.tensor_scalar(rs2[:], mv[:, :, 1], EPS, None, ALU.add).then_inc(S("var"), 1)
            dve.wait_ge(S("sd"), 1)
            link(dve.reciprocal(rs[:], rs[:]))
            for t in range(NT + 1):
                r = rows(t)
                v = uv[0:r, t, W:2 * W]
                link(dve.tensor_scalar(v, v, mv[0:r, t, 0:1], rs[0:r, t:t + 1], ALU.subtract, ALU.mult))
                link(dve.tensor_tensor(v, v, gbB[0:r, 0, :], ALU.mult))
                link(dve.tensor_tensor(v, v, gbB[0:r, 1, :], ALU.add))
            dve.sem_inc(S("v_done"), 1)
            for g in range(4):
                dve.wait_ge(S("band_mm"), g + 1)
                u = uv[:, 0:NT, 64 * g:64 * g + 64]
                dve.scalar_tensor_tensor(u, ps[:, 6 + g % 2, :].rearrange("p (t c) -> p t c", t=NT),
                                         bsp[:, g:g + 1], u, ALU.add, ALU.mult).then_inc(S("ob"), 1)
            for g in range(4):
                link(dve.tensor_scalar(st_s[0:NB, 64 * g:64 * g + 64], uv[0:NB, NT, W + 64 * g:W + 64 * g + 64],
                                       swb[0:NB, 0, g:g + 1], swb[0:NB, 1, g:g + 1], ALU.mult, ALU.add))
            dve.tensor_tensor(uv[0:NB, NT, 0:W], uv[0:NB, NT, 0:W], st_s[0:NB, :], ALU.mult).then_inc(S("ob"), 1)

            def to_oT(n_branch, sem_in, sem_out):
                for t in range(NT + 1):
                    r = rows(t)
                    dve.wait_ge(S(sem_in), t + 1)
                    dst = oT[:, n_branch, :, t * P:t * P + r] if n_branch is not None else dT[:, :, t * P:t * P + r]
                    dve.tensor_copy(dst, ps[:, 4 + t % 2, 0:2 * P].rearrange("p (f r) -> p f r", f=2)[:, :, 0:r]
                                    ).then_inc(S(sem_out), 1)

            dve.wait_ge(S("tb_out"), 16)
            to_oT(1, "ob_tr", "obT")

            def qk_evict(chunk, first=1, last=8):
                for i in range(first, last + 1):
                    t = TILE_ORDER[i]
                    dve.wait_ge(S(f"qk_tr_{chunk}"), i)
                    if i == 1 and chunk == "qka":
                        dve.wait_ge(S("out_vb"), 16)
                    src = ps[:, 4 + t % 2, :].rearrange("p (f r) -> p f r", f=4)
                    dve.tensor_scalar(qT[:, :, t * P:(t + 1) * P], src[:, 0:2, :], SCALE, None, ALU.mult)
                    link(dve.tensor_copy(kT[:, :, t * P:(t + 1) * P], src[:, 2:4, :]))
                    dve.sem_inc(S(f"qkT_{chunk}"), 1)

            qk_evict("qka")
            dve.wait_ge(S("evicted"), 27)
            fz = fa[:].rearrange("p t h -> p t h")
            link(dve.tensor_tensor(fz, fz, bfb[:].rearrange("p (o h) -> p o h", o=1).to_broadcast([P, NT + 1, H]), ALU.add))
            link(dve.tensor_scalar(faz[:], fa[:], -1.0, None, ALU.mult))
            dve.tensor_tensor(faz[:], faz[:], fa[:], ALU.max).then_inc(S("faz"), 1)
            dve.wait_ge(S("softplus"), 2)
            link(dve.scalar_tensor_tensor(lf[:], fa[:], 0.0, fal[:], ALU.min, ALU.subtract))
            dve.sem_inc(S("lf"), 1)
            link(dve.memset(lpre[:, 0, :], 0.0))
            for t in range(1, NT):
                link(dve.tensor_tensor(lpre[:, t, :], lpre[:, t - 1, :], lf[:, t - 1, :], ALU.add))
            dve.sem_inc(S("lpre"), 1)
            for n in range(8):
                dve.wait_ge(S("fb_mm"), n + 1)
                dve.tensor_copy(fb[:, n // 2, (n % 2) * 512:(n % 2) * 512 + 512], ps[:, 6 + n % 2, :]).then_inc(S("fb"), 1)

            def attention(br, bias_of, side):
                def shifted(n):
                    qt, h = items[n]
                    L = P * (qt + 1)
                    dve.wait_ge(S("sc"), 32 * br + n + 1)
                    src = ps[:, 2 * (n % 2):2 * (n % 2) + 2, :].rearrange("p a b -> p (a b)")[:, 0:L]
                    dve.tensor_tensor_reduce(out=p_sb[:, n % 2, 0:L], in0=src, in1=bias_of(h, qt), scale=-1.0,
                                             scalar=3.0e38, op0=ALU.add, op1=ALU.min,
                                             accum_out=am[:, n % 4:n % 4 + 1]).then_inc(S("sc_free"), 1)

                def blocks(n):
                    qt, h = items[n]
                    if qt >= 4:
                        dve.wait_ge(S("pt1"), PT_USES[br][n][1] + 1)
                        if n >= 2:
                            dve.wait_ge(S("pv"), 32 * br + n - 1)
                        w = P * (qt + 1) - 512
                        dve.tensor_copy(p_T[:, n % 2, 512:512 + w], ps[:, 5, 0:w]).then_inc(S("pt_free1"), 1)

                def norm(n):
                    qt, h = items[n]
                    dve.wait_ge(S("ex"), 32 * br + n + 1)
                    link(dve.reciprocal(arec[:, n % 4:n % 4 + 1], asum[:, n % 4:n % 4 + 1]))
                    dve.wait_ge(S("pv"), 32 * br + n + 1)
                    if n == 0:
                        for u in range(2):
                            dve.wait_ge(S(f"st{u}"), 16 * (NT // 2) * (br + 1))
                    if h == 0 and qt >= 2:
                        dve.wait_ge(S("ot"), NT * br + qt - 1)
                    dve.tensor_scalar(o_nat[:, qt % 2, h * 64:h * 64 + 64], ps[:, 6 + n % 2, 0:64],
                                      arec[:, n % 4:n % 4 + 1], None, ALU.mult).then_inc(S("on"), 1)

                shifted(0)
                shifted(1)
                for n in range(32):
                    blocks(n)
                    if n + 2 < 32:
                        shifted(n + 2)
                    norm(n)
                    side(n)

            def key_sums(s):
                b, half = s // 2, s % 2
                nr = 8 + half
                dve.wait_ge(S("kq"), s + 1)
                dve.tensor_reduce(sA[:, b, half * 8:half * 8 + nr, :],
                                  kv[:, half, 0:nr, :].rearrange("p r (h d) -> p r h d", h=H),
                                  AX.X, ALU.add).then_inc(S("ks"), 1)

            def key_sums_c(b):
                dve.wait_ge(S("kq"), 16 + b + 1)
                dve.tensor_reduce(sC[:, b, :, :], kv[:, b % 2, 5:9, :].rearrange("p r (h d) -> p r h d", h=H),
                                  AX.X, ALU.add).then_inc(S("ks"), 1)

            def side_a(n):
                if n % 2 == 1 and n // 2 < 16:
                    key_sums(n // 2)

            attention(0, lambda h, qt: fb[:, h, 0:P * (qt + 1)], side_a)
            link(dve.memset(wpb[:], 0.0))
            dve.sem_inc(S("wpb0"), 1)
            dve.wait_ge(S("lfg"), 16 * NB)
            link(dve.memset(lfs[:, :, :, 15, :], 0.0))
            link(dve.tensor_copy(lfs[:, 0, :, 0:15, :], lfg[:, :, 1:16, :]))
            cur = 0
            for d in (1, 2, 4, 8):
                dve.tensor_copy(lfs[:, 1 - cur, :, 16 - d:16, :], lfs[:, cur, :, 16 - d:16, :])
                link(dve.tensor_tensor(lfs[:, 1 - cur, :, 0:16 - d, :], lfs[:, cur, :, 0:16 - d, :],
                                       lfs[:, cur, :, d:16, :], ALU.add))
                cur = 1 - cur
            assert cur == 0
            dve.tensor_tensor(ltot[:].rearrange("p (b h) -> p b h", b=NB), lfs[:, 0, :, 0, :], lfg[:, :, 0, :],
                              ALU.add).then_inc(S("ltot"), 1)
            dve.wait_ge(S("lgb"), 16)
            dve.wait_ge(S("lsuf"), 1)
            link(dve.tensor_tensor(ltot[:], ps[:, 6, 0:32], lgb[:], ALU.add))
            dve.sem_inc(S("ba"), 1)
            link(dve.tensor_tensor(lfs[:, 0], lfs[:, 0],
                                   ltot[:].rearrange("p (b o h) -> p b o h", b=NB, o=1).to_broadcast([P, NB, 16, H]), ALU.add))
            dve.wait_ge(S("ks"), 16)
            s16 = sA[:, :, 0:16, :]
            link(dve.scalar_tensor_tensor(s16, s16, SCALE, lfs[:, 0], ALU.mult, ALU.add))
            link(dve.tensor_scalar(sA[:, :, 16, :], sA[:, :, 16, :], SCALE, bNew[:, 0:1], ALU.mult, ALU.add))

            def decode_softmax(br, s, before_total, between):
                n = s.shape[2]
                v = s[:].rearrange("p b r h -> p b h r")
                mxv = mx[:, 0:32].rearrange("p (b h) -> p b h", b=NB)
                dve.tensor_reduce(mxv, v, AX.X, ALU.max).then_inc(S("dmx"), 1)
                dve.wait_ge(S("dmx_tr"), br + 1)
                dve.tensor_reduce(mcol[0:32, :], ps[0:32, 6, 0:P], AX.X, ALU.max).then_inc(S("dmc"), 1)
                dve.wait_ge(S("dmb"), br + 1)
                link(dve.tensor_copy(mrow[:], ps[:, 6, P:P + 32]))
                mb = mrow[:].rearrange("p (b o h) -> p b o h", b=NB, o=1).to_broadcast([P, NB, n, H])
                dve.tensor_tensor(s[:], s[:], mb, ALU.subtract).then_inc(S("dsh"), 1)
                dve.wait_ge(S("dex"), br + 1)
                dve.tensor_reduce(dsum[:].rearrange("p (b h) -> p b h", b=NB), v, AX.X, ALU.add).then_inc(S("dsum"), 1)
                before_total()
                dve.wait_ge(S("dtot"), br + 1)
                link(dve.reciprocal(drec[:], ps[:, 6, 2 * P:2 * P + 32]))
                between()
                rb = drec[:].rearrange("p (b o h) -> p b o h", b=NB, o=1).to_broadcast([P, NB, n, H])
                dve.tensor_tensor(s[:], s[:], rb, ALU.mult).then_inc(S("dp"), 1)

            def decode_out(br, n_dv):
                dve.wait_ge(S("dv"), n_dv)
                for f in range(2):
                    for hh in range(2):
                        src = ps[64 * hh:64 * hh + 64, 6 + f, 0:2 * NB].rearrange("p (b h) -> p b h", h=2)[:, :, hh]
                        m = dve.tensor_copy(oT[64 * hh:64 * hh + 64, 2 * br, f, SEQ:TOK], src)
                link(m)
                dve.sem_inc(S("so"), 1)

            decode_softmax(0, sA, lambda: qk_evict("qkc", 1, 1), lambda: None)
            qk_evict("qkc", 2, 8)
            decode_out(0, 16)
            dve.wait_ge(S("spool"), 32)
            for g, w in enumerate(WINDOWS):
                v = spool[0:NB, 16 - w:16, 64 * g:64 * g + 64].rearrange("p w c -> p c w")
                link(dve.tensor_reduce(sd[0:NB, 64 * g:64 * g + 64], v, AX.X, ALU.add))
                link(dve.scalar_tensor_tensor(sd[0:NB, 64 * g:64 * g + 64], sd[0:NB, 64 * g:64 * g + 64], 1.0 / w,
                                              spool[0:NB, 15, 64 * g:64 * g + 64], ALU.mult, ALU.subtract))
            dve.wait_ge(S("out_pool"), 16)
            for g in range(4):
                dve.wait_ge(S("band_mm"), 4 + g + 1)
                dve.tensor_copy(vp[:, :, W + 64 * g:W + 64 * g + 64],
                                ps[:, g % 2, :].rearrange("p (t c) -> p t c", t=NT)).then_inc(S("dn"), 1)
            dve.sem_inc(S("dn"), 1)
            to_oT(None, "d_tr", "dT")
            def split_x(k):
                link(dve.tensor_copy(xH[:, k, :], xT[:, k, :]))
                dve.tensor_tensor(xL[:, k, :], xT[:, k, :], xH[:, k, :].bitcast(F32), ALU.subtract)

            def split_o(lo, hi):
                link(dve.tensor_copy(oH[:, :, :, lo:hi], oT[:, :, :, lo:hi]))
                link(dve.tensor_tensor(oL[:, :, :, lo:hi], oT[:, :, :, lo:hi], oH[:, :, :, lo:hi].bitcast(F32), ALU.subtract))

            attention(1, lambda h, qt: tb[:, h, SEQ - P - P * qt:SEQ],
                      lambda n: (key_sums_c(n // 4) if n % 4 == 3 else None, split_x(n // 3) if n < 24 and n % 3 == 1 else None))
            dve.wait_ge(S("ks"), 24)
            link(dve.tensor_scalar(sC[:], sC[:], SCALE, None, ALU.mult))
            link(dve.tensor_tensor(sC[:], sC[:], bC[:].rearrange("p (o r) h -> p o r h", o=1).to_broadcast([P, NB, 4, H]), ALU.add))
            decode_softmax(1, sC, lambda: None, lambda: None)
            dve.wait_ge(S("ot"), 2 * NT)
            dve.wait_ge(S("out_vc"), 16)
            split_o(0, SEQ)
            decode_out(1, 24)
            split_o(SEQ, TOK)
            dve.sem_inc(S("so"), 1)
            emit_dve2(dve, link)

        @block.gpsimd
        def _(pool):
            def gather(dst, src, index, sem):
                return pool.indirect_dma_start(dst, None, src, bass.IndirectOffsetOnAxis(index, 0)).then_inc(S(sem), 16)

            pool.wait_ge(S("idx"), 1)
            for b in range(NB):
                gather(lfg[:, b].rearrange("p r h -> p (r h)"), a["cache_lf"], idx[:, b, 2:3], "lfg")

            def load_a(s, which):
                b, half = s // 2, s % 2
                gather(kv[:, half, 0:8, :].rearrange("p r w -> p (r w)"), a[f"cache_{which}"],
                       idx[:, b, half:half + 1], f"{which}dma{half}")
                if half:
                    lo = 256 if which == "k" else 512
                    pool.dma_start(kv[0:1, 1, 8, :], a["s_dram"][b:b + 1, lo:lo + W]).then_inc(S(f"{which}dma1"), 16)

            def load_c(b, which):
                buf = b % 2
                for n, (w, d) in enumerate(DILATED):
                    pool.dma_start(kv[:, buf, 5 + n, :], a[f"state_{which}"][b, PAST - w:PAST:d, :]
                                   ).then_inc(S(f"{which}dma{buf}"), 16)
                lo = 1028 if which == "k" else 1284
                pool.dma_start(kv[0:1, buf, 8, :], a["s_dram"][b:b + 1, lo:lo + W]).then_inc(S(f"{which}dma{buf}"), 16)

            def load_q(n, b, lo):
                if n >= 2:
                    pool.wait_ge(S("kq"), 2 * (n - 1) if n <= NB + 1 else 16 + n - 1 - NB)
                pool.dma_start(qb[:, n % 2, :], a["s_dram"][b:b + 1, lo:lo + W].to_broadcast([P, W])
                               ).then_inc(S(f"qd{n % 2}"), 16)

            def times_q(buf, r0, r1, n):
                k = kv[:, buf, r0:r1, :]
                q = qb[:, n % 2, :].rearrange("p (o w) -> p o w", o=1).to_broadcast([P, r1 - r0, W])
                pool.tensor_tensor(k, k, q, ALU.mult).then_inc(S("kq"), 1)

            pool.wait_ge(S("cleared"), 3)
            pool.wait_ge(S("sd_qka"), 16)
            load_q(0, 0, 0)
            load_a(0, "k")
            load_a(1, "k")
            for s in range(16):
                b, half = s // 2, s % 2
                if half == 0 and b + 1 < NB:
                    load_q(b + 1, b + 1, 0)
                pool.wait_ge(S(f"qd{b % 2}"), 16 * (b // 2 + 1))
                pool.wait_ge(S(f"kdma{half}"), 16 * (b + 1) * (1 + half))
                times_q(half, 0, 8 + half, b)
                if s + 2 < 16:
                    pool.wait_ge(S("ks"), s + 1)
                    load_a(s + 2, "k")
            pool.wait_ge(S("sd_vfa"), 16)
            for s in range(16):
                if s < 2:
                    pool.wait_ge(S("ks"), 15 + s)
                else:
                    pool.wait_ge(S("dv"), s - 1)
                load_a(s, "v")
            pool.wait_ge(S("sd_qkc"), 16)
            load_q(NB, 0, 772)
            for b in range(2):
                pool.wait_ge(S("dv"), 15 + b)
                load_c(b, "k")
            for b in range(NB):
                if b + 1 < NB:
                    load_q(NB + b + 1, b + 1, 772)
                pool.wait_ge(S(f"qd{b % 2}"), 64 + 16 * (b // 2 + 1))
                pool.wait_ge(S(f"kdma{b % 2}"), 16 * NB * (1 + b % 2) + 64 * (b // 2 + 1))
                times_q(b % 2, 5, 9, NB + b)
                if b + 2 < NB:
                    pool.wait_ge(S("ks"), 16 + b + 1)
                    load_c(b + 2, "k")
            pool.wait_ge(S("sd_vpd"), 16)
            for b in range(NB):
                if b < 2:
                    pool.wait_ge(S("ks"), 23 + b)
                else:
                    pool.wait_ge(S("dv"), 16 + b - 1)
                load_c(b, "v")
            emit_pool2(pool)


def placed(nc, name, shape, dt, offset):
    class _C:
        def __enter__(self):
            return nc.alloc_sbuf_tensor_at(name, shape, dt, offset=offset, align_bytes=16)

        def __exit__(self, *_):
            return False
    return _C()


def buckets(dist):
    exact, longest = NBUCK // 2, 2048
    d = np.maximum(dist, 1).astype(np.float32)
    large = exact + (np.log(d / exact) / np.log(longest / exact) * (NBUCK - exact)).astype(np.int32)
    large = np.minimum(large, NBUCK - 1)
    return np.where(dist < exact, dist, large).astype(np.int32)


def constants():
    f = np.float32
    i, j = np.arange(P)[None, :], np.arange(P)[:, None]
    c = {"ident": np.eye(P, dtype=f), "tri_neg": -(j <= i).astype(f), "tri_after": (j > i).astype(f),
         "tril_T": (j <= i).astype(f), "causal": np.where(i <= j, 0, NEG).astype(f), "before": (j < i).astype(f)}
    rev = np.zeros((NBUCK + 1, TBW), f)
    for u in range(TBW):
        d = SEQ - 1 - u
        n = sum(0 <= d <= w and d % s == 0 for w, s in DILATED)
        if n:
            rev[buckets(np.array(d)), u] = 1
        rev[NBUCK, u] = math.log(n) if n else NEG
    dec = np.zeros((NBUCK + 1, 4, P), f)
    for n, (w, s) in enumerate(DILATED):
        dec[buckets(w - s * np.arange(P)), n, np.arange(P)] = 1
    dec[0, 3, 0] = 1
    dec[NBUCK, 3, 0] = math.log(len(DILATED))
    dec[NBUCK, 3, 1:] = NEG
    bands = np.zeros((P, 4, 3, P), f)
    for g, w in enumerate(WINDOWS):
        near = (j <= i) & (j > i - w)
        bands[:, g, 0] = np.where(near, 1 / np.minimum(w, i + 1), 0) - (i == j)
        bands[:, g, 1] = np.where(near, 1 / w, 0) - (i == j)
        bands[:, g, 2] = np.where(j - P > i - w, 1 / w, 0)
    p = np.arange(P)
    c |= {"oh_rev": rev, "oh_dec": dec, "bands": bands, "new_mask": np.where(p == 0, 0, NEG).astype(f)[:, None],
          "row_group": np.stack([p % 8 * 2, p % 8 * 2 + 1, p % 8, p * 0], 1).astype(f),
          "token": np.minimum(p[:, None] + P * np.arange(NT + 1), TOK - 1).astype(np.int32),
          "valid": (p[:, None] + P * np.arange(NT + 1) < TOK).astype(f),
          "tileno": np.tile(np.arange(MOE_TILES, dtype=f), (P, 1))}
    return c


def split_k(w):
    return w.reshape(-1, P, w.shape[-1]).transpose(1, 0, 2)


OUTS = {"y_p": (SEQ, D), "y_s": (NB, D), "k_a_p": (SEQ, W), "v_a_p": (SEQ, W), "lf_p": (SEQ, H), "k_a_s": (NB, W),
        "v_a_s": (NB, W), "lf_s": (NB, H), "k_c_p": (SEQ, W), "v_c_p": (SEQ, W), "k_c_s": (NB, W), "v_c_s": (NB, W),
        "pool_p": (15, W), "pd_s": (NB, W), "vb_s": (NB, W)}
SHAPES = {"y_p": (1, SEQ, D), "y_s": (NB, 1, D), "k_a_p": (1, 1, NT, P, H, HD), "v_a_p": (1, 1, NT, P, H, HD),
          "lf_p": (1, 1, NT, P, H), "k_a_s": (1, NB, 1, H, HD), "v_a_s": (1, NB, 1, H, HD), "lf_s": (1, NB, 1, H),
          "k_c_p": (1, 1, SEQ, H, HD), "v_c_p": (1, 1, SEQ, H, HD), "k_c_s": (1, NB, 1, H, HD),
          "v_c_s": (1, NB, 1, H, HD), "pool_p": (1, 1, 15, W), "pd_s": (1, NB, 1, W), "vb_s": (1, NB, 1, W)}
SCRATCH = {"s_dram": ((NB, SW), F32), "tb_dram": ((H, P * TBW), F32), "x1": ((TOK, D), F32), "ids": ((SLOTS, 1), I32),
           "yd": ((SLOTS, D), F32)}


def lay_out(v):
    v = {k: np.asarray(x) for k, x in v.items()}
    x = np.concatenate([v["x_prompt"].reshape(SEQ, D), v["x_sample"].reshape(NB, D)])
    n_pool = v["cache_k_a"].shape[1]
    wg = v["w_gate"][0].reshape(KD, P, 4, KD, P).transpose(3, 2, 1, 0, 4).reshape(KD, 4, P, -1)
    bg = v["b_gate"][0].reshape(4, KD, P).transpose(1, 0, 2)[..., None]
    wb = v["w_branch"][0].reshape(4, 2, P, KD, P).transpose(3, 0, 2, 1, 4).reshape(KD, 4, P, -1)
    w13 = np.concatenate([v[n][0].reshape(NE, KD, P, FE).transpose(0, 2, 1, 3) for n in ("w1", "w3")], -1)
    arrays = {
        "x": x, "xT": split_k(np.ascontiguousarray(x.T)), "w_in": split_k(v["w_in"][0]),
        "w_merge": np.concatenate([wg, wb, bg], -1).reshape(4 * KD, P, WM + 1), "w_out": split_k(v["w_out"][0]), "w_router": split_k(v["w_router"]),
        "w13": w13.reshape(NE, P, -1), "w2": v["w2"][0].reshape(NE, 2, P, D).transpose(0, 2, 1, 3).reshape(NE, P, -1),
        "pool_scale": v["pool_scale"][0].reshape(2, P).T, "w_pool": v["w_pool"][0],
        "w_spatial": v["w_spatial"][0].transpose(2, 0, 1), "b_spatial": v["b_spatial"][0].T,
        "w_spatial_00": v["w_spatial"][0][:, 0, 0][None], "b_spatial_0": v["b_spatial"][0][:, 0][None],
        "b_forget": v["b_forget"], "sgu_ln_g": v["sgu_ln_g"], "sgu_ln_b": v["sgu_ln_b"], "t5_table": v["t5_table"],
        "ln1_g": v["ln1_g"], "ln1_b": v["ln1_b"], "ln2_g": v["ln2_g"], "ln2_b": v["ln2_b"],
        "b_router": v["b_router"][None], "cache_k": v["cache_k_a"].reshape(n_pool * 16, -1),
        "cache_v": v["cache_v_a"].reshape(n_pool * 16, -1), "cache_lf": v["cache_logf_a"].reshape(n_pool * 8, -1),
        "state_k": v["state_k_c"].reshape(NB, PAST, W), "state_v": v["state_v_c"].reshape(NB, PAST, W),
        "state_pool": v["state_pool_d"][0], "page_rep": np.repeat(v["page_table"], 8, axis=1),
    }
    return {k: np.ascontiguousarray(x) for k, x in (arrays | constants()).items()}


def kernel(**inputs):
    from concourse import bacc
    from concourse.bass_utils import run_bass_kernel_spmd

    nc = bacc.Bacc("TRN2", target_bir_lowering=False, num_devices=1)
    arrays = lay_out(inputs)
    a = {k: nc.dram_tensor(f"in_{k}", x.shape, mybir.dt.from_np(x.dtype), kind="ExternalInput").ap()
         for k, x in arrays.items()}
    for k, shape in OUTS.items():
        a[k] = nc.dram_tensor(f"out_{k}", shape, F32, kind="ExternalOutput").ap()
    for k, (shape, dt) in SCRATCH.items():
        a[k] = nc.dram_tensor(f"tmp_{k}", shape, dt, kind="Internal").ap()
    build(nc, a)
    got = run_bass_kernel_spmd(nc, [{f"in_{k}": x for k, x in arrays.items()}], core_ids=[0]).results[0]
    return tuple(got[f"out_{k}"].reshape(SHAPES[k]) for k in OUTS)
```
